# Optimizing a Trainium2 kernel written in Bass

```python
import jax, jax.numpy as jnp
from jax import lax
import numpy as np

D_MODEL = 1024
BATCH = 1
SEQ = 512
DEPTH = 2

CHUNK = 64
N_MIXERS = 2
EPS = 1e-6

SSD_EXPAND = 2
SSD_D_INNER = SSD_EXPAND * D_MODEL
SSD_HEAD_DIM = 64
SSD_N_HEADS = SSD_D_INNER // SSD_HEAD_DIM
SSD_N_GROUPS = 8
SSD_HEADS_PER_GROUP = SSD_N_HEADS // SSD_N_GROUPS
SSD_D_STATE = 128
SSD_CONV_W = 4
SSD_BC_DIM = SSD_N_GROUPS * SSD_D_STATE
SSD_CONV_DIM = SSD_D_INNER + 2 * SSD_BC_DIM
SSD_IN_DIM = SSD_D_INNER + SSD_CONV_DIM + SSD_N_HEADS

SC_WIDTH = D_MODEL
SC_CONV_W = 3

FFN_HIDDEN = 2816
FFN_CONV_W = 3

N_SSD_LAYERS = (DEPTH + 1) // 2
N_SC_LAYERS = DEPTH // 2

kernel_name = "hybrid_ssd_shortconv_convffn_sandwich"

def rms_norm(x, g):
    xf = x.astype(jnp.float32)
    y = xf * lax.rsqrt(jnp.mean(xf * xf, axis=-1, keepdims=True) + EPS)
    return (y * g.astype(jnp.float32)).astype(x.dtype)

def causal_dwconv(x, w, b=None):
    k = w.shape[0]
    length = x.shape[1]
    xp = jnp.pad(x, ((0, 0), (k - 1, 0), (0, 0)))
    out = xp[:, 0:length] * w[0]
    for t in range(1, k):
        out = out + xp[:, t:t + length] * w[t]
    if b is not None:
        out = out + b
    return out

def ssd_scan(x, dt, a_head, b_in, c_in):
    bsz, length, h, p = x.shape
    g, n = b_in.shape[2], b_in.shape[3]
    r = h // g
    nc = length // CHUNK
    xf = (x.astype(jnp.float32) * dt[..., None]).reshape(bsz, nc, CHUNK, g, r, p)
    a = (dt * a_head).reshape(bsz, nc, CHUNK, g, r)
    a = jnp.moveaxis(a, 2, -1)
    a_cs = jnp.cumsum(a, axis=-1)
    bc = b_in.astype(jnp.float32).reshape(bsz, nc, CHUNK, g, n)
    cc = c_in.astype(jnp.float32).reshape(bsz, nc, CHUNK, g, n)
    seg = a_cs[..., :, None] - a_cs[..., None, :]
    tri = jnp.tril(jnp.ones((CHUNK, CHUNK), dtype=bool))
    lmat = jnp.exp(jnp.where(tri, seg, -jnp.inf))
    cb = jnp.einsum("bclgn,bcsgn->bcgls", cc, bc)
    y_diag = jnp.einsum("bcgls,bcgrls,bcsgrp->bclgrp", cb, lmat, xf)
    decay_states = jnp.exp(a_cs[..., -1:] - a_cs)
    states = jnp.einsum("bclgn,bcgrl,bclgrp->bcgrpn", bc, decay_states, xf)
    chunk_decay = jnp.exp(a_cs[..., -1])

    def step(s, inp):
        st, dec = inp
        return s * dec[..., None, None] + st, s

    init = jnp.zeros((bsz, g, r, p, n), jnp.float32)
    _, prev = lax.scan(step, init, (jnp.moveaxis(states, 1, 0), jnp.moveaxis(chunk_decay, 1, 0)))
    prev = jnp.moveaxis(prev, 0, 1)
    y_off = jnp.einsum("bclgn,bcgrpn,bcgrl->bclgrp", cc, prev, jnp.exp(a_cs))
    return (y_diag + y_off).reshape(bsz, length, h, p)

def ssd_mixer(h, w_in, conv_w, conv_b, dt_bias, a_log, d_skip, norm_w, w_out):
    bsz, length, _ = h.shape
    zxbcdt = h @ w_in
    z = zxbcdt[..., :SSD_D_INNER]
    xbc = zxbcdt[..., SSD_D_INNER:SSD_D_INNER + SSD_CONV_DIM]
    dt_raw = zxbcdt[..., SSD_D_INNER + SSD_CONV_DIM:]
    xbc = jax.nn.silu(causal_dwconv(xbc, conv_w, conv_b))
    xs = xbc[..., :SSD_D_INNER].reshape(bsz, length, SSD_N_HEADS, SSD_HEAD_DIM)
    bs = xbc[..., SSD_D_INNER:SSD_D_INNER + SSD_BC_DIM].reshape(bsz, length, SSD_N_GROUPS, SSD_D_STATE)
    cs = xbc[..., SSD_D_INNER + SSD_BC_DIM:].reshape(bsz, length, SSD_N_GROUPS, SSD_D_STATE)
    dt = jax.nn.softplus(dt_raw.astype(jnp.float32) + dt_bias.astype(jnp.float32))
    a_head = -jnp.exp(a_log.astype(jnp.float32))
    y = ssd_scan(xs, dt, a_head, bs, cs)
    y = y + xs.astype(jnp.float32) * d_skip.astype(jnp.float32)[:, None]
    y = y.reshape(bsz, length, SSD_D_INNER).astype(h.dtype)
    y = rms_norm(y * jax.nn.silu(z), norm_w)
    return y @ w_out

def shortconv_mixer(h, w_in, conv_w, w_out):
    bcv = h @ w_in
    gb = bcv[..., :SC_WIDTH]
    gc = bcv[..., SC_WIDTH:2 * SC_WIDTH]
    v = bcv[..., 2 * SC_WIDTH:]
    u = causal_dwconv(gc * v, conv_w)
    return (gb * u) @ w_out

def conv_ffn(h, w_up, conv_w, conv_b, w_down):
    up = h @ w_up
    gate = causal_dwconv(up[..., :FFN_HIDDEN], conv_w, conv_b)
    val = up[..., FFN_HIDDEN:]
    return (jax.nn.silu(gate) * val) @ w_down

def setup_inputs(seed: int = 0) -> dict:
    key = jax.random.key(seed)
    ks = jax.random.split(key, 20)
    f32 = jnp.float32
    nrm = lambda k, shape, s: jax.random.normal(k, shape, f32) * s
    x = jax.random.normal(ks[0], (BATCH, SEQ, D_MODEL), f32)
    gains = lambda k: 1.0 + nrm(k, (DEPTH, D_MODEL), 0.02)
    dt0 = jnp.exp(jax.random.uniform(ks[8], (N_SSD_LAYERS, SSD_N_HEADS), f32,
                                     np.float32(np.log(1e-3)), np.float32(np.log(1e-1))))
    return {
        "x": x,
        "mix_pre_g": gains(ks[1]),
        "mix_post_g": gains(ks[2]),
        "ffn_pre_g": gains(ks[3]),
        "ffn_post_g": gains(ks[4]),
        "ssd_w_in": nrm(ks[5], (N_SSD_LAYERS, D_MODEL, SSD_IN_DIM), D_MODEL ** -0.5),
        "ssd_conv_w": nrm(ks[6], (N_SSD_LAYERS, SSD_CONV_W, SSD_CONV_DIM), SSD_CONV_W ** -0.5),
        "ssd_conv_b": nrm(ks[7], (N_SSD_LAYERS, SSD_CONV_DIM), 0.01),
        "ssd_dt_bias": dt0 + jnp.log(-jnp.expm1(-dt0)),
        "ssd_A_log": jnp.log(jax.random.uniform(ks[9], (N_SSD_LAYERS, SSD_N_HEADS), f32, 1.0, 16.0)),
        "ssd_D": 1.0 + nrm(ks[10], (N_SSD_LAYERS, SSD_N_HEADS), 0.1),
        "ssd_norm_w": 1.0 + nrm(ks[11], (N_SSD_LAYERS, SSD_D_INNER), 0.02),
        "ssd_w_out": nrm(ks[12], (N_SSD_LAYERS, SSD_D_INNER, D_MODEL), SSD_D_INNER ** -0.5),
        "sc_w_in": nrm(ks[13], (N_SC_LAYERS, D_MODEL, 3 * SC_WIDTH), D_MODEL ** -0.5),
        "sc_conv_w": nrm(ks[14], (N_SC_LAYERS, SC_CONV_W, SC_WIDTH), SC_CONV_W ** -0.5),
        "sc_w_out": nrm(ks[15], (N_SC_LAYERS, SC_WIDTH, D_MODEL), SC_WIDTH ** -0.5),
        "ffn_w_up": nrm(ks[16], (DEPTH, D_MODEL, 2 * FFN_HIDDEN), D_MODEL ** -0.5),
        "ffn_conv_w": nrm(ks[17], (DEPTH, FFN_CONV_W, FFN_HIDDEN), FFN_CONV_W ** -0.5),
        "ffn_conv_b": nrm(ks[18], (DEPTH, FFN_HIDDEN), 0.01),
        "ffn_w_down": nrm(ks[19], (DEPTH, FFN_HIDDEN, D_MODEL), FFN_HIDDEN ** -0.5),
    }

def reference(x, mix_pre_g, mix_post_g, ffn_pre_g, ffn_post_g,
              ssd_w_in, ssd_conv_w, ssd_conv_b, ssd_dt_bias, ssd_A_log, ssd_D,
              ssd_norm_w, ssd_w_out, sc_w_in, sc_conv_w, sc_w_out,
              ffn_w_up, ffn_conv_w, ffn_conv_b, ffn_w_down):
    for i in range(DEPTH):
        j = i // N_MIXERS
        h = rms_norm(x, mix_pre_g[i])
        if i % N_MIXERS == 0:
            m = ssd_mixer(h, ssd_w_in[j], ssd_conv_w[j], ssd_conv_b[j], ssd_dt_bias[j],
                          ssd_A_log[j], ssd_D[j], ssd_norm_w[j], ssd_w_out[j])
        else:
            m = shortconv_mixer(h, sc_w_in[j], sc_conv_w[j], sc_w_out[j])
        x = x + rms_norm(m, mix_post_g[i])
        f = conv_ffn(rms_norm(x, ffn_pre_g[i]), ffn_w_up[i], ffn_conv_w[i], ffn_conv_b[i], ffn_w_down[i])
        x = x + rms_norm(f, ffn_post_g[i])
    return x


_drawn_inputs = setup_inputs


def setup_inputs(seed=0):
    import zlib

    import numpy as np

    out = dict(_drawn_inputs(seed))
    spreads = {}
    factors = {'ffn_post_g': 3.155, 'ssd_conv_b': 3.454, 'ffn_conv_b': 6.286}
    for name, (base, spread) in spreads.items():
        noise = np.random.default_rng([zlib.crc32(name.encode()), seed]).standard_normal(out[name].shape)
        drawn = base * np.exp(spread * noise) if base else spread * noise
        out[name] = __import__('jax').numpy.asarray(drawn.astype(out[name].dtype))
    for name, factor in factors.items():
        out[name] = (out[name] * factor).astype(out[name].dtype)
    return out
```

```python
from contextlib import ExitStack, contextmanager

import concourse.bass as bass
from concourse import mybir

F32 = mybir.dt.float32
F32R = mybir.dt.float32r
ALU = mybir.AluOpType
ACT = mybir.ActivationFunctionType

P = 128
EPS = 1e-6
KT = 8


class Tally:

    def __init__(self):
        self.start, self.count, self.per, self.i = 0, 0, 0, None

    def now(self):
        n = self.start + self.count
        return n if self.i is None else self.i * self.per + n

    def up(self, n=1):
        self.count += n
        return self.now()


@contextmanager
def turns(engine, first, end, per):
    for t in per:
        t.start, t.count = t.start + t.count - first * per[t], 0
    with engine.Fori(first, end) as i:
        for t, n in per.items():
            t.i, t.per = i, n
        yield i
        for n, t in enumerate(per):
            assert t.count == t.per, (n, t.count, t.per)
    for t in per:
        t.start, t.count, t.i = t.start + end * t.per, 0, None


def build(nc, x, mix_pre_g, mix_post_g, ffn_pre_g, ffn_post_g, ssd_w_in, ssd_conv_w, ssd_conv_b,
          ssd_dt_bias, ssd_A_log, ssd_D, ssd_norm_w, ssd_w_out, sc_w_in, sc_conv_w, sc_w_out,
          ffn_w_up, ffn_conv_w, ffn_conv_b, ffn_w_down, out):
    _, T, D = x.shape
    C = T // P
    DT = D // P
    DEPTH = mix_pre_g.shape[0]
    INNER = ssd_norm_w.shape[1]
    IT = INNER // P
    HEADS = ssd_D.shape[1]
    GROUPS = 8
    HG = HEADS // GROUPS
    XG = IT // GROUPS
    HX = HG // XG
    HD = P // HX
    STATE = P
    SSD_CW = ssd_conv_w.shape[1]
    CONV_T = ssd_conv_w.shape[2] // P
    W = sc_conv_w.shape[2]
    WT = W // P
    HIDDEN = ffn_conv_b.shape[1]
    FT = HIDDEN // P
    CW = ffn_conv_w.shape[1]
    DOWN = [KT, KT, FT - 2 * KT]
    LATER = T - P
    EXPS = 3 + XG * HX
    assert (T, D, C, DT, DEPTH, IT, FT, HD, CW, SSD_CW) == (512, 1024, 4, 8, 2, 16, 22, 64, 3, 4)

    def col_ssd_w(tap, t):
        return 0, tap * CONV_T + t

    def col_ssd_b(t):
        return 1, t

    GAINS = CONV_T

    def col_gain(which, layer, k):
        return 1, GAINS + which * DEPTH * DT + layer * DT + k

    NORM_W = GAINS + 4 * DEPTH * DT
    MIX_PRE, MIX_POST, FFN_PRE, FFN_POST = range(4)

    def col_norm_w(t):
        return 1, NORM_W + t

    def col_ffn_w(layer, tap, t):
        return 2 + layer, tap * FT + t

    def col_ffn_b(layer, t):
        return 2, CW * FT + layer * FT + t

    def col_sc_w(tap, t):
        return 3, CW * FT + tap * WT + t

    PAGES = [
        [(0, ssd_conv_w[0].rearrange("k (t p) -> (k t) p", p=P))],
        [(0, ssd_conv_b[0].rearrange("(t p) -> t p", p=P))]
        + [(GAINS + n * DEPTH * DT, g.rearrange("l (k p) -> (l k) p", p=P))
           for n, g in enumerate((mix_pre_g, mix_post_g, ffn_pre_g, ffn_post_g))]
        + [(NORM_W, ssd_norm_w[0].rearrange("(t p) -> t p", p=P))],
        [(0, ffn_conv_w[0].rearrange("k (t p) -> (k t) p", p=P)),
         (CW * FT, ffn_conv_b.rearrange("l (t p) -> (l t) p", p=P))],
        [(0, ffn_conv_w[1].rearrange("k (t p) -> (k t) p", p=P)),
         (CW * FT, sc_conv_w[0].rearrange("k (t p) -> (k t) p", p=P))],
    ]
    ROWS = [max(at + s.shape[0] for at, s in page) for page in PAGES]
    N_PARAM = sum(len(page) for page in PAGES)

    w_in = ssd_w_in[0].rearrange("(k p) n -> p k n", p=P)
    w_out = ssd_w_out[0].rearrange("(k p) n -> p k n", p=P)
    w_sc = sc_w_in[0].rearrange("(k p) n -> p k n", p=P)
    w_sc_out = sc_w_out[0].rearrange("(k p) n -> p k n", p=P)
    w_up = [ffn_w_up[l].rearrange("(k p) n -> p k n", p=P) for l in range(DEPTH)]
    w_down = [ffn_w_down[l].rearrange("(k p) n -> p k n", p=P) for l in range(DEPTH)]
    AT_X, AT_B = INNER, 2 * INNER
    AT_C = AT_B + GROUPS * STATE
    AT_DT = AT_C + GROUPS * STATE

    acs_dram = nc.dram_tensor("acs_dram", [HEADS, T], F32, kind="Internal").ap()

    ctx = ExitStack()
    with ctx:
        def sb(name, shape, dt=F32, stack=ctx):
            return stack.enter_context(nc.sbuf_tensor(name, shape, dt))

        def sem(name):
            return ctx.enter_context(nc.semaphore(name))

        bank = [ctx.enter_context(nc.psum_tensor(f"bank{n}", [P, 512], F32)) for n in range(8)]

        xs = sb("xs", [P, DT, T])
        h_hi, h_lo = sb("h_hi", [P, DT, T], F32R), sb("h_lo", [P, DT, T], F32R)
        w_raw = sb("w_raw", [P, 2, KT, P])
        w_hi, w_lo = sb("w_hi", [P, 2, KT, P], F32R), sb("w_lo", [P, 2, KT, P], F32R)
        ident, ones, tri = sb("ident", [P, P]), sb("ones", [P, P]), sb("tri", [P, P])
        par = sb("par", [P, 4, P])
        eps = sb("eps", [P, 1])
        r_post, r_pre, r_pre2 = sb("r_post", [P, T]), sb("r_pre", [P, T]), sb("r_pre2", [P, T])
        square, total = sb("square", [P, T]), sb("total", [P, T])

        with ExitStack() as start:
            x_tok = sb("x_tok", [P, C, D], stack=start)
            xn_tok = sb("xn_tok", [P, C, D], stack=start)
            pages = sb("pages", [P, 4, P], stack=start)
        with ExitStack() as ssd:
            y_hi, y_lo = sb("y_hi", [P, IT, T], F32R, ssd), sb("y_lo", [P, IT, T], F32R, ssd)
            acs_tok, dt_tok = sb("acs_tok", [P, C, HEADS], stack=ssd), sb("dt_tok", [P, C, HEADS], stack=ssd)
            d_col = sb("d_col", [P, IT], stack=ssd)
            acs_b = sb("acs_b", [P, HG, T], stack=ssd)
            mask = sb("mask", [P, HG, T], stack=ssd)
            feat = sb("feat", [P, 4, T], stack=ssd)
            pad = sb("pad", [P, 2, SSD_CW - 1 + T], stack=ssd)
            cbm = sb("cbm", [P, T], stack=ssd)
            b_tok = sb("b_tok", [P, LATER], stack=ssd)
            xdt = sb("xdt", [P, C, HG * HD], stack=ssd)
            xdd = sb("xdd", [P, C - 1, HG * HD], stack=ssd)
            prev = sb("prev", [P, C - 1, HG * HD], stack=ssd)
            e_row = sb("e_row", [P, XG, LATER], stack=ssd)
            z_act = sb("z_act", [P, XG, T], stack=ssd)
            decay, c_decay = sb("decay", [P, HG, C - 1], stack=ssd), sb("c_decay", [P, HG, C - 1], stack=ssd)
        with ExitStack() as small:
            sb("under", [P, 2 * IT * T + 2 * C * HEADS + IT], stack=small)
            wdt_raw = sb("wdt_raw", [P, DT, HEADS], stack=small)
            wdt_hi = sb("wdt_hi", [P, DT, HEADS], F32R, small)
            wdt_lo = sb("wdt_lo", [P, DT, HEADS], F32R, small)
            a_log_b, dt_bias_b, d_b = (sb(n, [P, HEADS], stack=small) for n in ("a_log_b", "dt_bias_b", "d_b"))
            sum_sq, r_tok = sb("sum_sq", [P, C], stack=small), sb("r_tok", [P, C], stack=small)
            dt_u, dt_e, a_tok = (sb(n, [P, C * HEADS], stack=small) for n in ("dt_u", "dt_e", "a_tok"))
            acs_row = sb("acs_row", [HEADS, T], stack=small)
        with ExitStack() as rest:
            hid_hi, hid_lo = sb("hid_hi", [P, FT, T], F32R, rest), sb("hid_lo", [P, FT, T], F32R, rest)
            m = sb("m", [P, DT, T], stack=rest)
            cpad = sb("cpad", [P, CW - 1 + T], stack=rest)
            acc, side, gated = (sb(n, [P, T], stack=rest) for n in ("acc", "side", "gated"))
        with ExitStack() as end:
            out_tok = sb("out_tok", [P, C, D], stack=end)

        x_landed = [sem(f"x_landed{c}") for c in range(C)]
        params_landed, small_landed = sem("params_landed"), sem("small_landed")
        raw_landed = [sem("raw_landed0"), sem("raw_landed1")]
        acs_stored, acs_landed, out_stored = sem("acs_stored"), sem("acs_landed"), sem("out_stored")
        w_hi_done, w_lo_done, unit_done = sem("w_hi_done"), sem("w_lo_done"), sem("unit_done")
        consts_done, x_squared, r_tok_root, r_tok_done = (sem(n) for n in ("consts_done", "x_squared", "r_tok_root", "r_tok_done"))
        xn_ready = sem("xn_ready")
        xn_done, x_turned, pages_turned, par_done = (sem(n) for n in ("xn_done", "x_turned", "pages_turned", "par_done"))
        dt_mm, dt_act, dt_vec, acs_mm, acs_row_done, acs_tok_done, wdt_split = (
            sem(n) for n in ("dt_mm", "dt_act", "dt_vec", "acs_mm", "acs_row_done", "acs_tok_done", "wdt_split"))
        h_hi_done, h_lo_done, evicted, pads_done = sem("h_hi_done"), sem("h_lo_done"), sem("evicted"), sem("pads_done")
        seg_done, exps_done, conv_step, silu_done = sem("seg_done"), sem("exps_done"), sem("conv_step"), sem("silu_done")
        cb_turned, b_tok_done, mask_step = sem("cb_turned"), sem("b_tok_done"), sem("mask_step")
        x_tok_turned, xdt_done, states_mm, prev0_done, state_step = (
            sem(n) for n in ("x_tok_turned", "xdt_done", "states_mm", "prev0_done", "state_step"))
        y_mm, y_step, y_hi_done, y_lo_done, scan_done = (sem(n) for n in ("y_mm", "y_step", "y_hi_done", "y_lo_done", "scan_done"))
        squared, summed, norm_mm, root_done, rstd_done = (sem(n) for n in ("squared", "summed", "norm_mm", "root_done", "rstd_done"))
        m_done, scaled_done, x_done = sem("m_done"), sem("scaled_done"), sem("x_done")
        gate_in, acc_done, side_step, hid_hi_done, hid_lo_done = (
            sem(n) for n in ("gate_in", "acc_done", "side_step", "hid_hi_done", "hid_lo_done"))
        out_turned, out_ready = sem("out_turned"), sem("out_ready")

        def one(page_col):
            return par[:, page_col[0], bass.ds(page_col[1], 1)]

        block = ctx.enter_context(nc.Block())

        @block.sync
        def _(sp):
            lo = Tally()

            def load(src, kt=KT, slot=0, free=True):
                n = lo.up()
                if free:
                    sp.wait_ge(w_lo_done, n - 2)
                sp.dma_start(w_raw[:, slot, 0:kt, :], src).then_inc(raw_landed[slot], 16)

            for c in range(C):
                sp.dma_start(x_tok[:, c, :], x[0, c * P:(c + 1) * P, :]).then_inc(x_landed[c], 16)
            for n, page in enumerate(PAGES):
                for at, src in page:
                    sp.dma_start(pages[at:at + src.shape[0], n, :], src).then_inc(params_landed, 16)
            sp.dma_start(wdt_raw[:], w_in[:, :, AT_DT:AT_DT + HEADS]).then_inc(small_landed, 16)
            sp.dma_start(a_log_b[:], ssd_A_log[0].partition_broadcast(P)).then_inc(small_landed, 16)
            sp.dma_start(dt_bias_b[:], ssd_dt_bias[0].partition_broadcast(P)).then_inc(small_landed, 16)
            sp.dma_start(d_b[:], ssd_D[0].partition_broadcast(P)).then_inc(small_landed, 16)

            def group_loads(g, first):
                load(w_in[:, :, bass.ds(g * P + (AT_B - P), P)], slot=0, free=not first)
                load(w_in[:, :, bass.ds(g * P + (AT_C - P), P)], slot=1, free=not first)
                if first:
                    sp.wait_ge(acs_stored, 16)
                    sp.wait_ge(acs_tok_done, 1)
                sp.wait_ge(exps_done, EXPS * g + (1 - EXPS))
                sp.dma_start(acs_b[:], acs_dram[bass.ds(g * HG - HG, HG), :].partition_broadcast(P)).then_inc(acs_landed, 16)
                for j in range(XG):
                    load(w_in[:, :, bass.ds(g * (XG * P) + (AT_X + (j - XG) * P), P)], slot=j % 2)
                for j in range(XG):
                    load(w_in[:, :, bass.ds(g * (XG * P) + (j - XG) * P, P)], slot=j % 2)

            group_loads(1, True)
            with turns(sp, 2, GROUPS + 1, {lo: 6}) as g:
                group_loads(g, False)
            with turns(sp, 1, DT + 1, {lo: 2}) as o:
                for half in range(2):
                    load(w_out[:, half * KT:(half + 1) * KT, bass.ds((o - 1) * P, P)], slot=half)
            for layer in range(DEPTH):
                if layer == 1:
                    with turns(sp, 1, WT // 2 + 1, {lo: 6}) as i:
                        for n, part in enumerate((1, 2, 0, 1, 2, 0)):
                            load(w_sc[:, :, bass.ds(i * (2 * P) + ((n // 3 - 2) * P + part * W), P)], slot=n % 2)
                    with turns(sp, 1, DT // 2 + 1, {lo: 2}) as i:
                        for n in range(2):
                            load(w_sc_out[:, :, bass.ds(i * (2 * P) + (n - 2) * P, P)], slot=n)
                with turns(sp, 1, FT + 1, {lo: 2}) as t:
                    for n in range(2):
                        load(w_up[layer][:, :, bass.ds(t * P + (n * HIDDEN - P), P)], slot=n)
                with turns(sp, 1, DT // 2 + 1, {lo: 6}) as i:
                    for n in range(6):
                        part = n % 3
                        load(w_down[layer][:, part * KT:part * KT + DOWN[part], bass.ds(i * (2 * P) + (n // 3 - 2) * P, P)],
                             DOWN[part], slot=n % 2)
            for half in range(2):
                sp.wait_ge(out_ready, (half + 1) * DT // 2)
                cols = slice(half * D // 2, (half + 1) * D // 2)
                sp.dma_start(out[0].rearrange("(c p) n -> p c n", p=P)[:, :, cols], out_tok[:, :, cols]).then_inc(out_stored, 16)
            sp.wait_ge(out_stored, 32)



        @block.gpsimd
        def _(pool):
            pool.memset(eps[:], EPS).then_inc(consts_done, 1)
            pool.memset(ones[:], 1.0).then_inc(consts_done, 1)
            pool.wait_ge(consts_done, 2)
            pool.affine_select(out=ident[:], in_=ones[:], compare_op=ALU.is_equal, fill=0.0, base=0,
                               pattern=[[-1, P]], channel_multiplier=1).then_inc(consts_done, 1)
            pool.affine_select(out=tri[:], in_=ones[:], compare_op=ALU.is_ge, fill=0.0, base=0,
                               pattern=[[1, P]], channel_multiplier=-1).then_inc(consts_done, 1)
            pool.wait_ge(acs_row_done, 1)
            pool.dma_start(acs_dram, acs_row[:]).then_inc(acs_stored, 16)
            done, sq = Tally(), Tally()
            norms = 0
            for tiles in [IT, DT] + [DT, DT] * 3:
                if norms:
                    pool.wait_ge(norm_mm, norms)
                pool.memset(total[:], 0.0).then_inc(summed, 1)
                done.up()
                with turns(pool, 0, tiles, {done: 1, sq: 1}):
                    pool.wait_ge(squared, sq.up())
                    pool.wait_ge(summed, done.now())
                    pool.tensor_tensor(total[:], total[:], square[:], ALU.add).then_inc(summed, 1)
                    done.up()
                norms += 1

        @block.scalar
        def _(act):
            hi, lands, units = Tally(), [Tally(), Tally()], Tally()
            sq, conv, silu, acc_n, gate_n = Tally(), Tally(), Tally(), Tally(), Tally()
            xd, mm_norm, side = Tally(), Tally(), Tally()

            def split(kt=KT):
                slot = hi.count % 2
                n = hi.up()
                act.wait_ge(raw_landed[slot], 16 * lands[slot].up())
                if units.i is not None or units.now() > 0:
                    act.wait_ge(unit_done, units.now())
                nc.scalar.activation(w_hi[:, slot, 0:kt, :], w_raw[:, slot, 0:kt, :], ACT.Copy).then_inc(w_hi_done, 1)

            def unit_ends(kt=KT):
                units.up()
                if kt:
                    split(kt)
                else:
                    act.wait_ge(unit_done, units.now())

            SPLITS = {hi: 1, units: 1, lands[0]: 0.5, lands[1]: 0.5}

            def per(n, **more):
                return {t: int(k * n) for t, k in SPLITS.items()}

            def square_of(src):
                act.wait_ge(summed, sq.up())
                nc.scalar.activation(square[:], src, ACT.Square).then_inc(squared, 1)

            def root(dst, n):
                act.wait_ge(norm_mm, mm_norm.up())
                nc.scalar.activation(dst, bank[7][:], ACT.Sqrt, bias=eps[:], scale=1.0 / n).then_inc(root_done, 1)

            for c in range(C):
                act.wait_ge(x_landed[c], 16)
                nc.scalar.activation(xn_tok[:, c, :], x_tok[:, c, :], ACT.Square, accum_out=sum_sq[:, c:c + 1]).then_inc(x_squared, 1)
            act.wait_ge(consts_done, 1)
            act.wait_ge(x_squared, C)
            nc.scalar.activation(r_tok[:], sum_sq[:], ACT.Sqrt, bias=eps[:], scale=1.0 / D).then_inc(r_tok_root, 1)
            act.wait_ge(pages_turned, 1)
            for n in range(4):
                last = nc.scalar.copy(par[:, n, 0:ROWS[n]], bank[6][:, n * P:n * P + ROWS[n]])
            last.then_inc(par_done, 1)
            act.wait_ge(small_landed, 64)
            nc.scalar.activation(wdt_hi[:], wdt_raw[:], ACT.Copy).then_inc(wdt_split, 1)
            act.wait_ge(par_done, 1)
            for k in range(DT):
                act.wait_ge(xn_done, k + 1)
                nc.scalar.activation(h_hi[:, k, :], bank[2 + k % 4][:], ACT.Copy, scale=one(col_gain(MIX_PRE, 0, k))).then_inc(h_hi_done, 1)
            split()
            split()
            act.wait_ge(dt_vec, 1)
            nc.scalar.activation(dt_e[:], dt_u[:], ACT.Abs).then_inc(dt_act, 1)
            act.wait_ge(dt_act, 1)
            nc.scalar.activation(dt_e[:], dt_e[:], ACT.Exp, scale=-1.0).then_inc(dt_act, 1)
            nc.scalar.activation(a_log_b[:], a_log_b[:], ACT.Exp).then_inc(dt_act, 1)
            act.wait_ge(dt_act, 3)
            nc.scalar.activation(dt_e[:], dt_e[:], ACT.Ln, bias=1.0).then_inc(dt_act, 1)
            for k in range(DT):
                act.wait_ge(x_turned, k + 1)
                nc.scalar.copy(xs[:, k, :], bank[k % 2][:]).then_inc(evicted, 1)
            act.wait_ge(acs_mm, 1)
            nc.scalar.copy(acs_row[:], bank[7][0:HEADS, :]).then_inc(acs_row_done, 1)
            act.wait_ge(acs_row_done, 1)
            nc.scalar.copy(decay[:, 0, 0:1], eps[:]).then_inc(exps_done, 1)
            act.wait_ge(pads_done, 1)

            def conv_in(slot, page_tile, f):
                unit_ends()
                if slot is not None:
                    act.wait_ge(conv_step, conv.now())
                u = mm_of(f)
                nc.scalar.copy(pad[:, f % 2, SSD_CW - 1:], u)
                nc.scalar.activation(feat[:, f, :], u, ACT.Identity, bias=one(col_ssd_b(page_tile)),
                                     scale=one(col_ssd_w(SSD_CW - 1, page_tile))).then_inc(evicted, 1)

            def conv_out(f):
                act.wait_ge(conv_step, conv.up(SSD_CW - 1))
                nc.scalar.activation(feat[:, f, :], feat[:, f, :], ACT.Silu).then_inc(silu_done, 1)

            def mm_of(n):
                return bank[n % 2][:]

            seg, bt, st, ymm, yst = Tally(), Tally(), Tally(), Tally(), Tally()
            exps = Tally()
            exps.up()
            with turns(act, 0, GROUPS, per(6) | {conv: 12, seg: 1, bt: 2, st: 2, yst: 10, sq: 2, exps: EXPS}) as g:
                conv_in(None, CONV_T - 2 * GROUPS + g, 0)
                act.wait_ge(seg_done, seg.up())
                nc.scalar.activation(mask[:], mask[:], ACT.Exp).then_inc(exps_done, 1)
                for j in range(XG):
                    for h in range(HX):
                        rows = slice(h * HD, (h + 1) * HD)
                        nc.scalar.activation(e_row[rows, j, :], acs_b[rows, j * HX + h, P:], ACT.Exp).then_inc(exps_done, 1)
                nc.scalar.activation(decay[:], decay[:], ACT.Exp).then_inc(exps_done, 1)
                nc.scalar.activation(c_decay[:], acs_b[:].rearrange("p h (c l) -> p h c l", l=P)[:, :, 0:C - 1, P - 1],
                                     ACT.Exp).then_inc(exps_done, 1)
                exps.up(EXPS)
                conv_in(None, CONV_T - GROUPS + g, 1)
                conv_out(0)
                conv_in(0, g * XG, 2)
                conv_out(1)
                conv_in(0, g * XG + 1, 3)
                conv_out(2)
                act.wait_ge(cb_turned, bt.up(2))
                nc.scalar.copy(b_tok[:], bank[3][:, 0:LATER]).then_inc(b_tok_done, 1)
                conv_out(3)
                for j in range(XG):
                    unit_ends()
                    nc.scalar.activation(z_act[:, j, :], bank[j % 2][:], ACT.Silu).then_inc(evicted, 1)
                act.wait_ge(states_mm, st.up())
                nc.scalar.copy(prev[:, 0, :], bank[6][:, 0:HG * HD]).then_inc(prev0_done, 1)
                st.up()
                for j in range(XG):
                    act.wait_ge(y_step, yst.up(4))
                    nc.scalar.activation(y_hi[:, bass.ds(g * XG + j, 1), :], feat[:, 2 + j, :], ACT.Copy,
                                         scale=one(col_norm_w(g * XG + j))).then_inc(y_hi_done, 1)
                    square_of(feat[:, 2 + j, :])
                    yst.up()

            md = Tally()

            def out_proj(o, first):
                for j in range(2):
                    unit_ends()
                    unit_ends()
                    if first and j == 0:
                        root(r_post[:], INNER)
                    act.wait_ge(m_done, md.up())
                    square_of(m[:, bass.ds(2 * o + j, 1), :])

            sq.up()
            out_proj(0, True)
            with turns(act, 1, DT // 2, per(4) | {md: 2, sq: 2}) as o:
                out_proj(o, False)

            def boundary(layer, which):
                root(r_post[:], D)
                sq.up()
                with turns(act, 0, DT, {xd: 1, sq: 1}) as k:
                    act.wait_ge(x_done, xd.up())
                    act.wait_ge(summed, sq.up())
                    nc.scalar.activation(h_hi[:, bass.ds(k, 1), :], xs[:, bass.ds(k, 1), :], ACT.Copy,
                                         scale=one(col_gain(which, layer, k))).then_inc(h_hi_done, 1)
                    nc.scalar.activation(square[:], xs[:, bass.ds(k, 1), :], ACT.Square).then_inc(squared, 1)

            def ffn_up(layer, t, first):
                for j in range(2):
                    unit_ends()
                    if first and j == 0:
                        root(r_pre[:], D)
                    act.wait_ge(gate_in, gate_n.up())
                    nc.scalar.activation(acc[:], cpad[:, CW - 1:], ACT.Identity, bias=one(col_ffn_b(layer, 2 * t + j)),
                                         scale=one(col_ffn_w(layer, CW - 1, 2 * t + j))).then_inc(acc_done, 1)
                    act.wait_ge(conv_step, conv.up(CW - 1))
                    nc.scalar.activation(acc[:], acc[:], ACT.Silu).then_inc(silu_done, 1)
                    unit_ends()
                    act.wait_ge(side_step, side.up(2))
                    nc.scalar.activation(hid_hi[:, bass.ds(2 * t + j, 1), :], gated[:], ACT.Copy).then_inc(hid_hi_done, 1)

            def ffn_down(o, last):
                for j in range(2):
                    unit_ends(DOWN[2])
                    unit_ends(0 if last and j else DOWN[0])
                    unit_ends(0 if last and j else DOWN[1])
                    nc.scalar.copy(m[:, bass.ds(2 * o + j, 1), :], bank[4 + j][:]).then_inc(m_done, 1)
                    md.up()
                    square_of(bank[4 + j][:])

            for layer in range(DEPTH):
                if layer == 1:
                    boundary(1, MIX_PRE)

                    def sc_in(i, first):
                        for j in range(2):
                            unit_ends()
                            if first and j == 0:
                                root(r_pre[:], D)
                            unit_ends()
                            act.wait_ge(gate_in, gate_n.up())
                            nc.scalar.activation(acc[:], cpad[:, CW - 1:], ACT.Copy,
                                                 scale=one(col_sc_w(CW - 1, 2 * i + j))).then_inc(acc_done, 1)
                            unit_ends()
                            conv.up(CW - 1)
                            act.wait_ge(side_step, side.up(3))
                            nc.scalar.activation(hid_hi[:, bass.ds(2 * i + j, 1), :], gated[:], ACT.Copy).then_inc(hid_hi_done, 1)

                    sc_in(0, True)
                    with turns(act, 1, WT // 2, per(6) | {gate_n: 2, conv: 4, side: 6}) as i:
                        sc_in(i, False)
                    sq.up()
                    with turns(act, 0, DT // 4, per(4) | {md: 4, sq: 4}) as i:
                        for j in range(4):
                            unit_ends()
                            nc.scalar.copy(m[:, bass.ds(4 * i + j, 1), :], bank[j][:]).then_inc(m_done, 1)
                            md.up()
                            square_of(bank[j][:])
                boundary(layer, FFN_PRE)
                ffn_up(layer, 0, True)
                with turns(act, 1, FT // 2, per(4) | {gate_n: 2, conv: 4, side: 4}) as t:
                    ffn_up(layer, t, False)
                sq.up()
                last_turn = 1 if layer == DEPTH - 1 else 0
                with turns(act, 0, DT // 2 - last_turn, per(6) | {md: 2, sq: 2}) as o:
                    ffn_down(o, False)
                if last_turn:
                    ffn_down(DT // 2 - 1, True)
            root(r_post[:], D)
            for k in range(DT):
                act.wait_ge(out_turned, k + 1)
                nc.scalar.copy(out_tok[:, :, k * P:(k + 1) * P], bank[k % 4][:].rearrange("p (c l) -> p c l", l=P)).then_inc(out_ready, 1)

        @block.vector
        def _(dve):
            lo, units = Tally(), Tally()
            ev, cs, hh, xdn, roots, rstd = Tally(), Tally(), Tally(), Tally(), Tally(), Tally()
            scaled, mdn = Tally(), Tally()

            def split(kt=KT):
                slot = lo.count % 2
                dve.wait_ge(w_hi_done, lo.up())
                nc.vector.tensor_tensor(w_lo[:, slot, 0:kt, :], w_raw[:, slot, 0:kt, :],
                                        w_hi[:, slot, 0:kt, :].bitcast(F32), ALU.subtract).then_inc(w_lo_done, 1)

            def unit_ends(kt=KT):
                units.up()
                if kt:
                    split(kt)

            def rstd_of(row):
                dve.wait_ge(root_done, roots.up())
                nc.vector.reciprocal(row, row).then_inc(rstd_done, 1)
                dve.wait_ge(rstd_done, rstd.up())

            dve.wait_ge(r_tok_root, 1)
            nc.vector.reciprocal(r_tok[:], r_tok[:]).then_inc(r_tok_done, 1)
            dve.wait_ge(r_tok_done, 1)
            for c in range(C):
                nc.vector.tensor_scalar(xn_tok[:, c, :], x_tok[:, c, :], r_tok[:, c:c + 1], None, ALU.mult).then_inc(xn_ready, 1)
            dve.wait_ge(wdt_split, 1)
            nc.vector.tensor_tensor(wdt_lo[:], wdt_raw[:], wdt_hi[:].bitcast(F32), ALU.subtract).then_inc(wdt_split, 1)
            dve.wait_ge(par_done, 1)
            for k in range(DT):
                dve.wait_ge(h_hi_done, hh.up())
                nc.vector.scalar_tensor_tensor(out=h_lo[:, k, :], in0=bank[2 + k % 4][:], scalar=one(col_gain(MIX_PRE, 0, k)),
                                               in1=h_hi[:, k, :].bitcast(F32), op0=ALU.mult, op1=ALU.subtract).then_inc(h_lo_done, 1)
            split()
            split()
            flat = "p (c h) -> p c h"
            dve.wait_ge(dt_mm, 1)
            nc.vector.tensor_tensor(dt_u[:].rearrange(flat, c=C), bank[6][:, 0:C * HEADS].rearrange(flat, c=C),
                                    dt_bias_b[:].unsqueeze(1).to_broadcast([P, C, HEADS]), ALU.add).then_inc(dt_vec, 1)
            dve.wait_ge(dt_act, 4)
            nc.vector.scalar_tensor_tensor(out=dt_tok[:].rearrange("p c h -> p (c h)"), in0=dt_u[:], scalar=0.0, in1=dt_e[:],
                                           op0=ALU.max, op1=ALU.add).then_inc(dt_vec, 1)
            dve.wait_ge(dt_vec, 2)
            nc.vector.scalar_tensor_tensor(out=a_tok[:].rearrange(flat, c=C), in0=dt_tok[:], scalar=-1.0,
                                           in1=a_log_b[:].unsqueeze(1).to_broadcast([P, C, HEADS]),
                                           op0=ALU.mult, op1=ALU.mult).then_inc(dt_vec, 1)
            nc.vector.memset(pad[:, :, 0:SSD_CW - 1], 0.0).then_inc(pads_done, 1)
            dve.wait_ge(small_landed, 64)
            for h in range(HX):
                nc.vector.tensor_copy(d_col[h * HD:(h + 1) * HD, :], d_b[h * HD:(h + 1) * HD, :].rearrange("p (t h) -> p h t", h=HX)[:, h, :])
            dve.wait_ge(acs_mm, 2)
            nc.vector.tensor_copy(acs_tok[:].rearrange("p c h -> p (c h)"), bank[6][:, 0:C * HEADS]).then_inc(acs_tok_done, 1)
            dve.wait_ge(acs_tok_done, 1)
            ev.up(DT)
            al, sd, ex, cb, ms, xt, st, p0, ss, ym, ys, yh = (Tally() for _ in range(12))
            ex.up()
            sd.up()

            def conv(f, page_tile):
                unit_ends()
                dve.wait_ge(evicted, ev.up())
                for tap in range(SSD_CW - 1):
                    if tap:
                        dve.wait_ge(conv_step, cs.now())
                    nc.vector.scalar_tensor_tensor(out=feat[:, f, :], in0=pad[:, f % 2, tap:tap + T],
                                                   scalar=one(col_ssd_w(tap, page_tile)), in1=feat[:, f, :],
                                                   op0=ALU.mult, op1=ALU.add).then_inc(conv_step, 1)
                    cs.up()

            def by_head(ap):
                return ap.rearrange("p (h e) -> p h e", e=HD)

            with turns(dve, 0, GROUPS, {lo: 6, units: 6, ev: 6, cs: 12, al: 1, sd: 1, ex: EXPS, cb: 1, ms: 2, xt: 2,
                                        st: 2, p0: 1, ss: 4, ym: 2, ys: 10, yh: 2}) as g:
                dve.wait_ge(acs_landed, 16 * al.up())
                nc.vector.tensor_tensor(decay[:], acs_b[:].rearrange("p h (c l) -> p h c l", l=P)[:, :, 0:C - 1, P - 1],
                                        acs_tok[:, 0:C - 1, bass.ds(g * HG, HG)].rearrange("p c h -> p h c"), ALU.subtract)
                dve.wait_ge(scan_done, sd.now())
                sd.up()
                for h in range(HG):
                    for c in range(C):
                        span = slice(c * P, (c + 1) * P)
                        last = nc.vector.tensor_scalar(mask[:, h, span], acs_b[:, h, span], acs_tok[:, c, bass.ds(g * HG + h, 1)],
                                                       0.0, ALU.subtract, ALU.min)
                last.then_inc(seg_done, 1)
                conv(0, CONV_T - 2 * GROUPS + g)
                conv(1, CONV_T - GROUPS + g)
                conv(2, g * XG)
                conv(3, g * XG + 1)
                dve.wait_ge(cb_turned, cb.now() * 2 + 1)
                cb.up()
                nc.vector.tensor_tensor(cbm[:].rearrange("p (c l) -> p c l", l=P), bank[2][:].rearrange("p (c l) -> p c l", l=P),
                                        tri[:].unsqueeze(1).to_broadcast([P, C, P]), ALU.mult).then_inc(mask_step, 1)
                dve.wait_ge(mask_step, ms.up())
                dve.wait_ge(exps_done, ex.up(EXPS))
                nc.vector.tensor_tensor(mask[:], mask[:], cbm[:].unsqueeze(1).to_broadcast([P, HG, T]), ALU.mult).then_inc(mask_step, 1)
                ms.up()
                unit_ends()
                for j in range(XG):
                    dve.wait_ge(x_tok_turned, xt.up())
                    nc.vector.tensor_tensor(
                        xdt[:, :, j * P:(j + 1) * P].rearrange("p c (h e) -> p c h e", e=HD),
                        bank[4 + j][:].rearrange("p (c h e) -> p c h e", c=C, e=HD),
                        dt_tok[:, :, bass.ds(g * HG + j * HX, HX)].unsqueeze(3).to_broadcast([P, C, HX, HD]),
                        ALU.mult).then_inc(xdt_done, 1)
                dve.wait_ge(xdt_done, (xt.now() // 2) * 3 - 1 if xt.i is None else xt.i * 3 + 2)
                nc.vector.tensor_tensor(
                    xdd[:].rearrange("p c (h e) -> p c h e", e=HD),
                    xdt[:, 0:C - 1, :].rearrange("p c (h e) -> p c h e", e=HD),
                    decay[:].rearrange("p h c -> p c h").unsqueeze(3).to_broadcast([P, C - 1, HG, HD]),
                    ALU.mult).then_inc(xdt_done, 1)
                unit_ends()
                dve.wait_ge(states_mm, st.up(2))
                dve.wait_ge(prev0_done, p0.up())
                for c in range(1, C - 1):
                    if c > 1:
                        dve.wait_ge(state_step, ss.now())
                    nc.vector.tensor_tensor(by_head(prev[:, c, :]), by_head(prev[:, c - 1, :]),
                                            c_decay[:, :, c:c + 1].to_broadcast([P, HG, HD]), ALU.mult).then_inc(state_step, 1)
                    dve.wait_ge(state_step, ss.up())
                    nc.vector.tensor_tensor(prev[:, c, :], prev[:, c, :],
                                            bank[6 + c // 2][:, c % 2 * HG * HD:(c % 2 + 1) * HG * HD], ALU.add).then_inc(state_step, 1)
                    ss.up()
                dve.wait_ge(evicted, ev.up(2))
                for j in range(XG):
                    dve.wait_ge(y_mm, ym.up())
                    nc.vector.tensor_tensor(e_row[:, j, :], e_row[:, j, :], bank[2 + j][:, P:], ALU.mult).then_inc(y_step, 1)
                    nc.vector.scalar_tensor_tensor(out=feat[:, 2 + j, :], in0=feat[:, 2 + j, :],
                                                   scalar=d_col[:, bass.ds(g * XG + j, 1)], in1=bank[4 + j][:],
                                                   op0=ALU.mult, op1=ALU.add).then_inc(y_step, 1)
                    dve.wait_ge(y_step, ys.up(2))
                    nc.vector.tensor_tensor(feat[:, 2 + j, P:], feat[:, 2 + j, P:], e_row[:, j, :], ALU.add).then_inc(y_step, 1)
                    dve.wait_ge(y_step, ys.up())
                    nc.vector.tensor_tensor(feat[:, 2 + j, :], feat[:, 2 + j, :], z_act[:, j, :], ALU.mult).then_inc(y_step, 1)
                    ys.up()
                    dve.wait_ge(y_hi_done, yh.up())
                    nc.vector.scalar_tensor_tensor(out=y_lo[:, bass.ds(g * XG + j, 1), :], in0=feat[:, 2 + j:3 + j, :],
                                                   scalar=one(col_norm_w(g * XG + j)), in1=y_hi[:, bass.ds(g * XG + j, 1), :].bitcast(F32),
                                                   op0=ALU.mult, op1=ALU.subtract).then_inc(y_step, 1)
                    ys.up()

            def out_proj(o, first):
                for j in range(2):
                    unit_ends()
                    unit_ends()
                    if first and j == 0:
                        rstd_of(r_post[:])
                    dve.wait_ge(unit_done, units.now())
                    nc.vector.tensor_tensor(m[:, bass.ds(2 * o + j, 1), :], bank[j][:].unsqueeze(1), r_post[:].unsqueeze(1),
                                            ALU.mult).then_inc(m_done, 1)
                    mdn.up()

            out_proj(0, True)
            with turns(dve, 1, DT // 2, {lo: 4, units: 4, mdn: 2}) as o:
                out_proj(o, False)

            def residual(layer, which, k):
                if xdn.i is not None:
                    dve.wait_ge(x_done, xdn.now())
                nc.vector.tensor_tensor(side[:].unsqueeze(1), m[:, bass.ds(k, 1), :], r_post[:].unsqueeze(1), ALU.mult).then_inc(scaled_done, 1)
                dve.wait_ge(scaled_done, scaled.up())
                nc.vector.scalar_tensor_tensor(out=xs[:, bass.ds(k, 1), :], in0=side[:].unsqueeze(1), scalar=one(col_gain(which, layer, k)),
                                               in1=xs[:, bass.ds(k, 1), :], op0=ALU.mult, op1=ALU.add).then_inc(x_done, 1)
                xdn.up()

            def boundary(post, pre):
                rstd_of(r_post[:])
                dve.wait_ge(m_done, mdn.now())

                def low(k):
                    dve.wait_ge(h_hi_done, hh.up())
                    nc.vector.scalar_tensor_tensor(out=h_lo[:, bass.ds(k, 1), :], in0=xs[:, bass.ds(k, 1), :],
                                                   scalar=one(col_gain(pre[1], pre[0], k)), in1=h_hi[:, bass.ds(k, 1), :].bitcast(F32),
                                                   op0=ALU.mult, op1=ALU.subtract).then_inc(h_lo_done, 1)

                residual(post[0], post[1], 0)
                with turns(dve, 1, DT, {scaled: 1, xdn: 1, hh: 1}) as k:
                    residual(post[0], post[1], k)
                    low(k - 1)
                low(DT - 1)

            hd, ac, sl, st2 = Tally(), Tally(), Tally(), Tally()
            sl.up(4 * GROUPS)

            def conv_taps(cols):
                dve.wait_ge(acc_done, ac.up())
                for tap in range(CW - 1):
                    if tap:
                        dve.wait_ge(conv_step, cs.now())
                    nc.vector.scalar_tensor_tensor(out=acc[:], in0=cpad[:, tap:tap + T], scalar=one(cols(tap)), in1=acc[:],
                                                   op0=ALU.mult, op1=ALU.add).then_inc(conv_step, 1)
                    cs.up()

            def low_hidden(t):
                dve.wait_ge(hid_hi_done, hd.up())
                nc.vector.tensor_tensor(hid_lo[:, bass.ds(t, 1), :], gated[:].unsqueeze(1), hid_hi[:, bass.ds(t, 1), :].bitcast(F32),
                                        ALU.subtract).then_inc(hid_lo_done, 1)

            def ffn_up(layer, t, first):
                for j in range(2):
                    unit_ends()
                    if first and j == 0:
                        rstd_of(r_pre[:])
                    dve.wait_ge(unit_done, units.now())
                    nc.vector.tensor_tensor(cpad[:, CW - 1:], bank[2 * j][:], r_pre[:], ALU.mult).then_inc(gate_in, 1)
                    conv_taps(lambda tap: col_ffn_w(layer, tap, 2 * t + j))
                    unit_ends()
                    dve.wait_ge(unit_done, units.now())
                    nc.vector.tensor_tensor(side[:], bank[2 * j + 1][:], r_pre[:], ALU.mult).then_inc(side_step, 1)
                    dve.wait_ge(side_step, st2.up())
                    dve.wait_ge(silu_done, sl.up())
                    nc.vector.tensor_tensor(gated[:], side[:], acc[:], ALU.mult).then_inc(side_step, 1)
                    st2.up()
                    low_hidden(2 * t + j)

            def sc_in(i, first):
                for j in range(2):
                    unit_ends()
                    if first and j == 0:
                        rstd_of(r_pre[:])
                        nc.vector.tensor_tensor(r_pre2[:], r_pre[:], r_pre[:], ALU.mult).then_inc(rstd_done, 1)
                        dve.wait_ge(rstd_done, rstd.up())
                    dve.wait_ge(unit_done, units.now())
                    nc.vector.tensor_tensor(side[:], bank[3 * j][:], r_pre2[:], ALU.mult).then_inc(side_step, 1)
                    dve.wait_ge(side_step, st2.up())
                    unit_ends()
                    dve.wait_ge(unit_done, units.now())
                    nc.vector.tensor_tensor(cpad[:, CW - 1:], side[:], bank[3 * j + 1][:], ALU.mult).then_inc(gate_in, 1)
                    conv_taps(lambda tap: col_sc_w(tap, 2 * i + j))
                    unit_ends()
                    dve.wait_ge(unit_done, units.now())
                    nc.vector.tensor_tensor(side[:], bank[3 * j + 2][:], r_pre[:], ALU.mult).then_inc(side_step, 1)
                    dve.wait_ge(side_step, st2.up())
                    dve.wait_ge(conv_step, cs.now())
                    nc.vector.tensor_tensor(gated[:], side[:], acc[:], ALU.mult).then_inc(side_step, 1)
                    st2.up()
                    low_hidden(2 * i + j)

            for layer in range(DEPTH):
                if layer == 1:
                    boundary((0, FFN_POST), (1, MIX_PRE))
                    sc_in(0, True)
                    with turns(dve, 1, WT // 2, {lo: 6, units: 6, cs: 4, ac: 2, hd: 2, st2: 6}) as i:
                        sc_in(i, False)
                    with turns(dve, 0, DT // 4, {lo: 4, units: 4}):
                        for j in range(4):
                            unit_ends()
                    mdn.up(DT)
                else:
                    nc.vector.memset(cpad[:, 0:CW - 1], 0.0).then_inc(pads_done, 1)
                    dve.wait_ge(pads_done, 2)
                boundary((layer, MIX_POST), (layer, FFN_PRE))
                ffn_up(layer, 0, True)
                with turns(dve, 1, FT // 2, {lo: 4, units: 4, cs: 4, ac: 2, hd: 2, st2: 4, sl: 2}) as t:
                    ffn_up(layer, t, False)
                last_turn = 1 if layer == DEPTH - 1 else 0
                with turns(dve, 0, DT // 2 - last_turn, {lo: 6, units: 6}):
                    for n in range(6):
                        unit_ends(DOWN[(n + 2) % 3])
                if last_turn:
                    for n in range(6):
                        unit_ends(DOWN[(n + 2) % 3] if n < 4 else 0)
                mdn.up(DT)
            rstd_of(r_post[:])
            dve.wait_ge(m_done, mdn.now())
            residual(1, FFN_POST, 0)
            with turns(dve, 1, DT, {scaled: 1, xdn: 1}) as k:
                residual(1, FFN_POST, k)

        @block.tensor
        def _(pe):
            lo, sm, hl, norms, xdn = Tally(), Tally(), Tally(), Tally(), Tally()

            def three(dst, wh, wl, xh, xl, start, stop):
                nc.tensor.matmul(dst, wh, xh, start=start, stop=False)
                nc.tensor.matmul(dst, wl, xh, start=False, stop=False)
                return nc.tensor.matmul(dst, wh, xl, start=False, stop=stop)

            def unit(dst, in_hi, in_lo, kt=KT, k0=0, start=True, stop=True, by_tile=False):
                slot = lo.count % 2
                pe.wait_ge(w_lo_done, lo.up())
                for k in range(kt):
                    if by_tile:
                        pe.wait_ge(h_lo_done, hl.up())
                    last = three(dst, w_hi[:, slot, k, :], w_lo[:, slot, k, :], in_hi[:, k0 + k, :], in_lo[:, k0 + k, :],
                                 start and k == 0, stop and k == kt - 1)
                last.then_inc(unit_done, 1)

            def norm(tiles):
                pe.wait_ge(summed, sm.up(tiles + 1))
                nc.tensor.matmul(bank[7][:], ones[:], total[:], start=True, stop=True).then_inc(norm_mm, 1)

            pe.wait_ge(consts_done, 4)
            pe.wait_ge(params_landed, 16 * N_PARAM)
            for n in range(4):
                last = nc.tensor.transpose(bank[6][:, n * P:n * P + ROWS[n]], pages[0:ROWS[n], n, :], ident[0:ROWS[n], 0:ROWS[n]])
            last.then_inc(pages_turned, 1)
            pe.wait_ge(xn_ready, C)
            for k in range(DT):
                if k >= 4:
                    pe.wait_ge(h_lo_done, k - 3)
                for c in range(C):
                    last = nc.tensor.transpose(bank[2 + k % 4][:, c * P:(c + 1) * P], xn_tok[:, c, k * P:(k + 1) * P], ident[:])
                last.then_inc(xn_done, 1)
            pe.wait_ge(par_done, 1)
            pe.wait_ge(wdt_split, 2)
            pe.wait_ge(h_lo_done, hl.up(DT))
            for c in range(C):
                for k in range(DT):
                    span = slice(c * P, (c + 1) * P)
                    last = three(bank[6][:, c * HEADS:(c + 1) * HEADS], h_hi[:, k, span], h_lo[:, k, span], wdt_hi[:, k, :],
                                 wdt_lo[:, k, :], k == 0, k == DT - 1)
            last.then_inc(dt_mm, 1)
            for k in range(DT):
                if k >= 2:
                    pe.wait_ge(evicted, k - 1)
                for c in range(C):
                    last = nc.tensor.transpose(bank[k % 2][:, c * P:(c + 1) * P], x_tok[:, c, k * P:(k + 1) * P], ident[:])
                last.then_inc(x_turned, 1)
            pe.wait_ge(dt_vec, 3)
            for c in range(C):
                last = nc.tensor.matmul(bank[7][0:HEADS, c * P:(c + 1) * P], a_tok[:, c * HEADS:(c + 1) * HEADS], tri[:],
                                        start=True, stop=True)
            last.then_inc(acs_mm, 1)
            nc.tensor.matmul(bank[6][:, 0:C * HEADS], tri[:], a_tok[:], start=True, stop=True).then_inc(acs_mm, 1)
            pe.wait_ge(acs_tok_done, 1)
            pe.wait_ge(acs_row_done, 1)
            nc.tensor.transpose(bank[7][:, 0:P], ident[:], ident[:]).then_inc(scan_done, 1)

            ev, si, bt, mk, xd, ss, ys = (Tally() for _ in range(7))
            ev.up(DT)

            def group_unit(n):
                pe.wait_ge(evicted, ev.up() - 2)
                unit(bank[n % 2][:], h_hi, h_lo)

            with turns(pe, 0, GROUPS, {lo: 6, ev: 6, si: 4, bt: 1, mk: 2, xd: 3, ss: 4}) as g:
                for n in range(4):
                    group_unit(n)
                pe.wait_ge(silu_done, si.up(2))
                for c in range(C):
                    span = slice(c * P, (c + 1) * P)
                    last = nc.tensor.matmul(bank[2][:, span], feat[:, 0, span], feat[:, 1, span], start=True, stop=True)
                last.then_inc(cb_turned, 1)
                for c in range(C - 1):
                    last = nc.tensor.transpose(bank[3][:, c * P:(c + 1) * P], feat[:, 0, c * P:(c + 1) * P], ident[:])
                last.then_inc(cb_turned, 1)
                group_unit(4)
                for j in range(XG):
                    pe.wait_ge(silu_done, si.up())
                    for c in range(C):
                        last = nc.tensor.transpose(bank[4 + j][:, c * P:(c + 1) * P], feat[:, 2 + j, c * P:(c + 1) * P], ident[:])
                    last.then_inc(x_tok_turned, 1)
                group_unit(5)
                pe.wait_ge(b_tok_done, bt.up())
                pe.wait_ge(xdt_done, xd.up(3))
                for c in range(C - 1):
                    last = nc.tensor.matmul(bank[6 + c // 2][:, c % 2 * HG * HD:(c % 2 + 1) * HG * HD], b_tok[:, c * P:(c + 1) * P],
                                            xdd[:, c, :], start=True, stop=True)
                    if c:
                        last.then_inc(states_mm, 1)
                pe.wait_ge(mask_step, mk.up(2))
                for j in range(XG):
                    for h in range(HX):
                        for c in range(C):
                            cols = slice(j * P + h * HD, j * P + (h + 1) * HD)
                            last = nc.tensor.matmul(bank[4 + j][h * HD:(h + 1) * HD, c * P:(c + 1) * P], xdt[:, c, cols],
                                                    mask[:, j * HX + h, c * P:(c + 1) * P], start=True, stop=True)
                last.then_inc(scan_done, 1)
                pe.wait_ge(prev0_done, bt.now())
                pe.wait_ge(state_step, ss.up(4))
                for j in range(XG):
                    for c in range(1, C):
                        last = nc.tensor.matmul(bank[2 + j][:, c * P:(c + 1) * P], prev[:, c - 1, j * P:(j + 1) * P],
                                                feat[:, 1, c * P:(c + 1) * P], start=True, stop=True)
                    last.then_inc(y_mm, 1)

            def out_proj(first):
                for j in range(2):
                    unit(bank[j][:], y_hi, y_lo, stop=False)
                    unit(bank[j][:], y_hi, y_lo, k0=KT, start=False)
                    if first and j == 0:
                        norm(IT)

            pe.wait_ge(evicted, ev.now())
            pe.wait_ge(y_step, 10 * GROUPS)
            out_proj(True)
            with turns(pe, 1, DT // 2, {lo: 4}):
                out_proj(False)

            def ffn_up(first):
                for j in range(2):
                    unit(bank[2 * j][:], h_hi, h_lo, by_tile=first and j == 0)
                    if first and j == 0:
                        norm(DT)
                    unit(bank[2 * j + 1][:], h_hi, h_lo)

            def sc_in(first):
                for j in range(2):
                    unit(bank[3 * j][:], h_hi, h_lo, by_tile=first and j == 0)
                    if first and j == 0:
                        norm(DT)
                    unit(bank[3 * j + 1][:], h_hi, h_lo)
                    unit(bank[3 * j + 2][:], h_hi, h_lo)

            hidden = 0
            for layer in range(DEPTH):
                norm(DT)
                if layer == 1:
                    sc_in(True)
                    with turns(pe, 1, WT // 2, {lo: 6}):
                        sc_in(False)
                    hidden += WT
                    pe.wait_ge(hid_lo_done, hidden)
                    with turns(pe, 0, DT // 4, {lo: 4}):
                        for j in range(4):
                            unit(bank[j][:], hid_hi, hid_lo)
                    norm(DT)
                ffn_up(True)
                with turns(pe, 1, FT // 2, {lo: 4}):
                    ffn_up(False)
                hidden += FT
                pe.wait_ge(hid_lo_done, hidden)
                with turns(pe, 0, DT // 2, {lo: 6}):
                    for j in range(2):
                        for n, kt in enumerate(DOWN):
                            unit(bank[4 + j][:], hid_hi, hid_lo, kt=kt, k0=n * KT, start=n == 0, stop=n == 2)
            norm(DT)
            for k in range(DT):
                pe.wait_ge(x_done, 3 * DT + k + 1)
                if k >= 4:
                    pe.wait_ge(out_ready, k - 3)
                for c in range(C):
                    last = nc.tensor.transpose(bank[k % 4][:, c * P:(c + 1) * P], xs[:, k, c * P:(c + 1) * P], ident[:])
                last.then_inc(out_turned, 1)


_INS = ["x", "mix_pre_g", "mix_post_g", "ffn_pre_g", "ffn_post_g", "ssd_w_in", "ssd_conv_w", "ssd_conv_b", "ssd_dt_bias",
        "ssd_A_log", "ssd_D", "ssd_norm_w", "ssd_w_out", "sc_w_in", "sc_conv_w", "sc_w_out", "ffn_w_up", "ffn_conv_w",
        "ffn_conv_b", "ffn_w_down"]


def kernel(**inputs):
    import numpy as np
    import concourse.bacc as bacc
    from concourse.bass_utils import run_bass_kernel_spmd

    nc = bacc.Bacc("TRN2", target_bir_lowering=False, num_devices=1)
    arrays, args = {}, []
    for name in _INS:
        a = np.ascontiguousarray(inputs[name])
        arrays[f"in_{name}"] = a
        args.append(nc.dram_tensor(f"in_{name}", a.shape, mybir.dt.from_np(a.dtype), kind="ExternalInput").ap())
    args.append(nc.dram_tensor("out_0", inputs["x"].shape, F32, kind="ExternalOutput").ap())
    build(nc, *args)
    r = run_bass_kernel_spmd(nc, [arrays], core_ids=[0])
    return r.results[0]["out_0"]
```

```python
from contextlib import ExitStack, contextmanager

import concourse.bass as bass
from concourse import mybir

F32 = mybir.dt.float32
F32R = mybir.dt.float32r
ALU = mybir.AluOpType
ACT = mybir.ActivationFunctionType

P = 128
EPS = 1e-6
KT = 8


class Tally:

    def __init__(self):
        self.start, self.count, self.per, self.i = 0, 0, 0, None

    def now(self):
        n = self.start + self.count
        return n if self.i is None else self.i * self.per + n

    def up(self, n=1):
        self.count += n
        return self.now()


@contextmanager
def turns(engine, first, end, per):
    for t in per:
        t.start, t.count = t.start + t.count - first * per[t], 0
    with engine.Fori(first, end) as i:
        for t, n in per.items():
            t.i, t.per = i, n
        yield i
        for n, t in enumerate(per):
            assert t.count == t.per, (n, t.count, t.per)
    for t in per:
        t.start, t.count, t.i = t.start + end * t.per, 0, None


def build(nc, x, mix_pre_g, mix_post_g, ffn_pre_g, ffn_post_g, ssd_w_in, ssd_conv_w, ssd_conv_b,
          ssd_dt_bias, ssd_A_log, ssd_D, ssd_norm_w, ssd_w_out, sc_w_in, sc_conv_w, sc_w_out,
          ffn_w_up, ffn_conv_w, ffn_conv_b, ffn_w_down, out):
    _, T, D = x.shape
    C = T // P
    DT = D // P
    DEPTH = mix_pre_g.shape[0]
    INNER = ssd_norm_w.shape[1]
    IT = INNER // P
    HEADS = ssd_D.shape[1]
    GROUPS = 8
    HG = HEADS // GROUPS
    XG = IT // GROUPS
    HX = HG // XG
    HD = P // HX
    STATE = P
    SSD_CW = ssd_conv_w.shape[1]
    CONV_T = ssd_conv_w.shape[2] // P
    W = sc_conv_w.shape[2]
    WT = W // P
    HIDDEN = ffn_conv_b.shape[1]
    FT = HIDDEN // P
    CW = ffn_conv_w.shape[1]
    DOWN = [KT, KT, FT - 2 * KT]
    LATER = T - P
    EXPS = 3 + XG * HX
    assert (T, D, C, DT, DEPTH, IT, FT, HD, CW, SSD_CW) == (512, 1024, 4, 8, 2, 16, 22, 64, 3, 4)

    def col_ssd_w(tap, t):
        return 0, tap * CONV_T + t

    def col_ssd_b(t):
        return 1, t

    GAINS = CONV_T

    def col_gain(which, layer, k):
        return 1, GAINS + which * DEPTH * DT + layer * DT + k

    NORM_W = GAINS + 4 * DEPTH * DT
    MIX_PRE, MIX_POST, FFN_PRE, FFN_POST = range(4)

    def col_norm_w(t):
        return 1, NORM_W + t

    def col_ffn_w(layer, tap, t):
        return 2 + layer, tap * FT + t

    def col_ffn_b(layer, t):
        return 2, CW * FT + layer * FT + t

    def col_sc_w(tap, t):
        return 3, CW * FT + tap * WT + t

    PAGES = [
        [(0, ssd_conv_w[0].rearrange("k (t p) -> (k t) p", p=P))],
        [(0, ssd_conv_b[0].rearrange("(t p) -> t p", p=P))]
        + [(GAINS + n * DEPTH * DT, g.rearrange("l (k p) -> (l k) p", p=P))
           for n, g in enumerate((mix_pre_g, mix_post_g, ffn_pre_g, ffn_post_g))]
        + [(NORM_W, ssd_norm_w[0].rearrange("(t p) -> t p", p=P))],
        [(0, ffn_conv_w[0].rearrange("k (t p) -> (k t) p", p=P)),
         (CW * FT, ffn_conv_b.rearrange("l (t p) -> (l t) p", p=P))],
        [(0, ffn_conv_w[1].rearrange("k (t p) -> (k t) p", p=P)),
         (CW * FT, sc_conv_w[0].rearrange("k (t p) -> (k t) p", p=P))],
    ]
    ROWS = [max(at + s.shape[0] for at, s in page) for page in PAGES]
    N_PARAM = sum(len(page) for page in PAGES)

    w_in = ssd_w_in[0].rearrange("(k p) n -> p k n", p=P)
    w_out = ssd_w_out[0].rearrange("(k p) n -> p k n", p=P)
    w_sc = sc_w_in[0].rearrange("(k p) n -> p k n", p=P)
    w_sc_out = sc_w_out[0].rearrange("(k p) n -> p k n", p=P)
    w_up = [ffn_w_up[l].rearrange("(k p) n -> p k n", p=P) for l in range(DEPTH)]
    w_down = [ffn_w_down[l].rearrange("(k p) n -> p k n", p=P) for l in range(DEPTH)]
    AT_X, AT_B = INNER, 2 * INNER
    AT_C = AT_B + GROUPS * STATE
    AT_DT = AT_C + GROUPS * STATE

    acs_dram = nc.dram_tensor("acs_dram", [HEADS, T], F32, kind="Internal").ap()

    ctx = ExitStack()
    with ctx:
        def sb(name, shape, dt=F32, stack=ctx):
            return stack.enter_context(nc.sbuf_tensor(name, shape, dt))

        def sem(name):
            return ctx.enter_context(nc.semaphore(name))

        bank = [ctx.enter_context(nc.psum_tensor(f"bank{n}", [P, 512], F32)) for n in range(8)]

        xs = sb("xs", [P, DT, T])
        h_hi, h_lo = sb("h_hi", [P, DT, T], F32R), sb("h_lo", [P, DT, T], F32R)
        w_raw = sb("w_raw", [P, 2, KT, P])
        w_hi, w_lo = sb("w_hi", [P, 2, KT, P], F32R), sb("w_lo", [P, 2, KT, P], F32R)
        ident, ones, tri = sb("ident", [P, P]), sb("ones", [P, P]), sb("tri", [P, P])
        par = sb("par", [P, 4, P])
        eps = sb("eps", [P, 1])
        r_post, r_pre, r_pre2 = sb("r_post", [P, T]), sb("r_pre", [P, T]), sb("r_pre2", [P, T])
        square, total = sb("square", [P, 2, T]), sb("total", [P, T])
        rms_tok = sb("rms_tok", [P, C])

        with ExitStack() as start:
            x_tok = sb("x_tok", [P, C, D], stack=start)
            xn_tok = sb("xn_tok", [P, C, D], stack=start)
            pages = sb("pages", [P, 4, P], stack=start)
        with ExitStack() as ssd:
            y_hi, y_lo = sb("y_hi", [P, IT, T], F32R, ssd), sb("y_lo", [P, IT, T], F32R, ssd)
            acs_tok, dt_tok = sb("acs_tok", [P, C, HEADS], stack=ssd), sb("dt_tok", [P, C, HEADS], stack=ssd)
            d_col = sb("d_col", [P, IT], stack=ssd)
            acs_b = sb("acs_b", [P, HG, T], stack=ssd)
            mask = sb("mask", [P, HG, T], stack=ssd)
            feat = sb("feat", [P, 4, T], stack=ssd)
            pad = sb("pad", [P, 2, SSD_CW - 1 + T], stack=ssd)
            cbm = sb("cbm", [P, T], stack=ssd)
            b_tok = sb("b_tok", [P, LATER], stack=ssd)
            xdt = sb("xdt", [P, C, HG * HD], stack=ssd)
            xdd = sb("xdd", [P, C - 1, HG * HD], stack=ssd)
            prev = sb("prev", [P, C - 1, HG * HD], stack=ssd)
            e_row = sb("e_row", [P, XG, LATER], stack=ssd)
            z_act = sb("z_act", [P, XG, T], stack=ssd)
            decay, c_decay = sb("decay", [P, HG, C - 1], stack=ssd), sb("c_decay", [P, HG, C - 1], stack=ssd)
        with ExitStack() as small:
            sb("under", [P, 2 * IT * T + 2 * C * HEADS + IT], stack=small)
            wdt_raw = sb("wdt_raw", [P, DT, HEADS], stack=small)
            wdt_hi, wdt_lo = sb("wdt_hi", [P, DT, P], F32R, small), sb("wdt_lo", [P, DT, P], F32R, small)
            dt_row = sb("dt_row", [HEADS, T], stack=small)
            a_log_b, dt_bias_b, d_b = (sb(n, [P, HEADS], stack=small) for n in ("a_log_b", "dt_bias_b", "d_b"))
            sum_sq, r_tok = sb("sum_sq", [P, C], stack=small), sb("r_tok", [P, C], stack=small)
            dt_u, dt_e, a_tok = (sb(n, [P, C * HEADS], stack=small) for n in ("dt_u", "dt_e", "a_tok"))
            acs_row = sb("acs_row", [HEADS, T], stack=small)
        with ExitStack() as rest:
            hid_hi, hid_lo = sb("hid_hi", [P, FT, T], F32R, rest), sb("hid_lo", [P, FT, T], F32R, rest)
            m = sb("m", [P, DT, T], stack=rest)
            cpad = sb("cpad", [P, CW - 1 + T], stack=rest)
            acc, gated, side = sb("acc", [P, T], stack=rest), sb("gated", [P, T], stack=rest), sb("side", [P, 2, T], stack=rest)
        with ExitStack() as end:
            out_tok = sb("out_tok", [P, C, D], stack=end)

        x_landed = [sem(f"x_landed{c}") for c in range(C)]
        params_landed, small_landed = sem("params_landed"), sem("small_landed")
        raw_landed = [sem("raw_landed0"), sem("raw_landed1")]
        acs_stored, acs_landed, out_stored = sem("acs_stored"), sem("acs_landed"), sem("out_stored")
        w_hi_done, w_lo_done, unit_done = sem("w_hi_done"), sem("w_lo_done"), sem("unit_done")
        consts_done, x_squared, r_tok_root, r_tok_done = (sem(n) for n in ("consts_done", "x_squared", "r_tok_root", "r_tok_done"))
        xn_ready = sem("xn_ready")
        xn_done, x_turned, pages_turned, par_done = (sem(n) for n in ("xn_done", "x_turned", "pages_turned", "par_done"))
        wdt_cleared, dt_row_mm, dt_row_done = sem("wdt_cleared"), sem("dt_row_mm"), sem("dt_row_done")
        dt_mm, dt_act, dt_vec, acs_mm, acs_row_done, acs_tok_done, wdt_split = (
            sem(n) for n in ("dt_mm", "dt_act", "dt_vec", "acs_mm", "acs_row_done", "acs_tok_done", "wdt_split"))
        h_hi_done, h_lo_done, evicted, xs_done, pads_done = (sem(n) for n in ("h_hi_done", "h_lo_done", "evicted", "xs_done", "pads_done"))
        seg_done, exps_done, conv_step, silu_done = sem("seg_done"), sem("exps_done"), sem("conv_step"), sem("silu_done")
        cb_turned, b_tok_done, mask_step = sem("cb_turned"), sem("b_tok_done"), sem("mask_step")
        x_tok_turned, xdt_done, states_mm, prev0_done, state_step = (
            sem(n) for n in ("x_tok_turned", "xdt_done", "states_mm", "prev0_done", "state_step"))
        y_mm, y_step, y_hi_done, y_lo_done, scan_done = (sem(n) for n in ("y_mm", "y_step", "y_hi_done", "y_lo_done", "scan_done"))
        squared, summed, norm_mm, root_done, rstd_done, row_mm, row_done, pre2_done = (
            sem(n) for n in ("squared", "summed", "norm_mm", "root_done", "rstd_done", "row_mm", "row_done", "pre2_done"))
        m_done, scaled_done, x_done = sem("m_done"), sem("scaled_done"), sem("x_done")
        gate_in, acc_done, side_step, hid_hi_done, hid_lo_done = (
            sem(n) for n in ("gate_in", "acc_done", "side_step", "hid_hi_done", "hid_lo_done"))
        out_turned, out_ready = sem("out_turned"), sem("out_ready")

        def one(page_col):
            return par[:, page_col[0], bass.ds(page_col[1], 1)]

        block = ctx.enter_context(nc.Block())

        @block.sync
        def _(sp):
            lo = Tally()

            def load(src, kt=KT, slot=0, free=True):
                n = lo.up()
                if free:
                    sp.wait_ge(w_lo_done, n - 2)
                sp.dma_start(w_raw[:, slot, 0:kt, :], src).then_inc(raw_landed[slot], 16)

            for c in range(C):
                sp.dma_start(x_tok[:, c, :], x[0, c * P:(c + 1) * P, :]).then_inc(x_landed[c], 16)
            for n, page in enumerate(PAGES):
                for at, src in page:
                    sp.dma_start(pages[at:at + src.shape[0], n, :], src).then_inc(params_landed, 16)
            sp.dma_start(wdt_raw[:], w_in[:, :, AT_DT:AT_DT + HEADS]).then_inc(small_landed, 16)
            sp.dma_start(a_log_b[:], ssd_A_log[0].partition_broadcast(P)).then_inc(small_landed, 16)
            sp.dma_start(dt_bias_b[:], ssd_dt_bias[0].partition_broadcast(P)).then_inc(small_landed, 16)
            sp.dma_start(d_b[:], ssd_D[0].partition_broadcast(P)).then_inc(small_landed, 16)

            def group_loads(g, first):
                load(w_in[:, :, bass.ds(g * P + (AT_B - P), P)], slot=0, free=not first)
                load(w_in[:, :, bass.ds(g * P + (AT_C - P), P)], slot=1, free=not first)
                if first:
                    sp.wait_ge(acs_stored, 16)
                    sp.wait_ge(acs_tok_done, 1)
                sp.wait_ge(exps_done, EXPS * g + (1 - EXPS))
                sp.dma_start(acs_b[:], acs_dram[bass.ds(g * HG - HG, HG), :].partition_broadcast(P)).then_inc(acs_landed, 16)
                for j in range(XG):
                    load(w_in[:, :, bass.ds(g * (XG * P) + (AT_X + (j - XG) * P), P)], slot=j % 2)
                for j in range(XG):
                    load(w_in[:, :, bass.ds(g * (XG * P) + (j - XG) * P, P)], slot=j % 2)

            group_loads(1, True)
            with turns(sp, 2, GROUPS + 1, {lo: 6}) as g:
                group_loads(g, False)
            with turns(sp, 1, DT + 1, {lo: 2}) as o:
                for half in range(2):
                    load(w_out[:, half * KT:(half + 1) * KT, bass.ds((o - 1) * P, P)], slot=half)
            for layer in range(DEPTH):
                if layer == 1:
                    with turns(sp, 1, WT // 2 + 1, {lo: 6}) as i:
                        for n, part in enumerate((1, 2, 0, 1, 2, 0)):
                            load(w_sc[:, :, bass.ds(i * (2 * P) + ((n // 3 - 2) * P + part * W), P)], slot=n % 2)
                    with turns(sp, 1, DT // 2 + 1, {lo: 2}) as i:
                        for n in range(2):
                            load(w_sc_out[:, :, bass.ds(i * (2 * P) + (n - 2) * P, P)], slot=n)
                with turns(sp, 1, FT + 1, {lo: 2}) as t:
                    for n in range(2):
                        load(w_up[layer][:, :, bass.ds(t * P + (n * HIDDEN - P), P)], slot=n)
                with turns(sp, 1, DT // 2 + 1, {lo: 6}) as i:
                    for n in range(6):
                        part = n % 3
                        load(w_down[layer][:, part * KT:part * KT + DOWN[part], bass.ds(i * (2 * P) + (n // 3 - 2) * P, P)],
                             DOWN[part], slot=n % 2)
            for half in range(2):
                sp.wait_ge(out_ready, (half + 1) * DT // 2)
                cols = slice(half * D // 2, (half + 1) * D // 2)
                sp.dma_start(out[0].rearrange("(c p) n -> p c n", p=P)[:, :, cols], out_tok[:, :, cols]).then_inc(out_stored, 16)
            sp.wait_ge(out_stored, 32)



        @block.gpsimd
        def _(pool):
            for part in (wdt_hi, wdt_lo):
                pool.memset(part[:].bitcast(F32)[:, :, HEADS:], 0.0).then_inc(wdt_cleared, 1)
            pool.memset(eps[:], EPS).then_inc(consts_done, 1)
            pool.memset(ones[:], 1.0).then_inc(consts_done, 1)
            pool.wait_ge(consts_done, 2)
            pool.affine_select(out=ident[:], in_=ones[:], compare_op=ALU.is_equal, fill=0.0, base=0,
                               pattern=[[-1, P]], channel_multiplier=1).then_inc(consts_done, 1)
            pool.affine_select(out=tri[:], in_=ones[:], compare_op=ALU.is_ge, fill=0.0, base=0,
                               pattern=[[1, P]], channel_multiplier=-1).then_inc(consts_done, 1)
            done, sq = Tally(), Tally()
            norms = 0
            for tiles in [IT, DT] + [DT, DT] * 3:
                if norms:
                    pool.wait_ge(norm_mm, norms)
                pool.memset(total[:], 0.0).then_inc(summed, 1)
                done.up()
                def add(n):
                    pool.wait_ge(squared, sq.up())
                    pool.wait_ge(summed, done.now())
                    pool.tensor_tensor(total[:], total[:], square[:, n, :], ALU.add).then_inc(summed, 1)
                    done.up()

                with turns(pool, 0, tiles // 2 - 1, {done: 2, sq: 2}):
                    add(0)
                    add(1)
                add(0)
                sq.up()
                norms += 1

        @block.scalar
        def _(act):
            hi, lands, units = Tally(), [Tally(), Tally()], Tally()
            sq, conv, silu, acc_n, gate_n = Tally(), Tally(), Tally(), Tally(), Tally()
            xd, mm_norm, side = Tally(), Tally(), Tally()

            def split(kt=KT):
                slot = hi.count % 2
                n = hi.up()
                act.wait_ge(raw_landed[slot], 16 * lands[slot].up())
                if units.i is not None or units.now() > 0:
                    act.wait_ge(unit_done, units.now())
                nc.scalar.activation(w_hi[:, slot, 0:kt, :], w_raw[:, slot, 0:kt, :], ACT.Copy).then_inc(w_hi_done, 1)

            def unit_ends(kt=KT):
                units.up()
                if kt:
                    split(kt)
                else:
                    act.wait_ge(unit_done, units.now())

            SPLITS = {hi: 1, units: 1, lands[0]: 0.5, lands[1]: 0.5}

            def per(n, **more):
                return {t: int(k * n) for t, k in SPLITS.items()}

            def square_of(src, n, ahead=1):
                act.wait_ge(summed, sq.up() - ahead)
                nc.scalar.activation(square[:, n % 2, :], src, ACT.Square).then_inc(squared, 1)

            def root(n):
                act.wait_ge(norm_mm, mm_norm.up())
                nc.scalar.activation(rms_tok[:], bank[6][:, 0:C], ACT.Sqrt, bias=eps[:], scale=1.0 / n).then_inc(root_done, 1)

            def keep_row(dst):
                act.wait_ge(row_mm, mm_norm.now())
                nc.scalar.copy(dst, bank[7][:]).then_inc(row_done, 1)

            act.wait_ge(consts_done, 1)
            for c in range(C):
                act.wait_ge(x_landed[c], 16)
                nc.scalar.activation(xn_tok[:, c, :], x_tok[:, c, :], ACT.Square, accum_out=sum_sq[:, c:c + 1]).then_inc(x_squared, 1)
                act.wait_ge(x_squared, c + 1)
                nc.scalar.activation(r_tok[:, c:c + 1], sum_sq[:, c:c + 1], ACT.Sqrt, bias=eps[:], scale=1.0 / D).then_inc(r_tok_root, 1)
            act.wait_ge(pages_turned, 1)
            for n in range(4):
                last = nc.scalar.copy(par[:, n, 0:ROWS[n]], bank[6][:, n * P:n * P + ROWS[n]])
            last.then_inc(par_done, 1)
            act.wait_ge(small_landed, 64)
            act.wait_ge(wdt_cleared, 2)
            nc.scalar.activation(wdt_hi[:, :, 0:HEADS], wdt_raw[:], ACT.Copy).then_inc(wdt_split, 1)
            act.wait_ge(par_done, 1)
            split()
            for k in range(DT):
                act.wait_ge(xn_done, k + 1)
                nc.scalar.activation(h_hi[:, k, :], bank[2 + k % 4][:], ACT.Copy, scale=one(col_gain(MIX_PRE, 0, k))).then_inc(h_hi_done, 1)
            split()
            act.wait_ge(dt_row_mm, 1)
            nc.scalar.copy(dt_row[:], bank[7][0:HEADS, :]).then_inc(dt_row_done, 1)
            act.wait_ge(dt_vec, 1)
            nc.scalar.activation(dt_e[:], dt_u[:], ACT.Abs).then_inc(dt_act, 1)
            act.wait_ge(dt_act, 1)
            nc.scalar.activation(dt_e[:], dt_e[:], ACT.Exp, scale=-1.0).then_inc(dt_act, 1)
            nc.scalar.activation(a_log_b[:], a_log_b[:], ACT.Exp).then_inc(dt_act, 1)
            act.wait_ge(dt_act, 3)
            nc.scalar.activation(dt_e[:], dt_e[:], ACT.Ln, bias=1.0).then_inc(dt_act, 1)
            act.wait_ge(acs_mm, 1)
            nc.scalar.copy(acs_row[:], bank[7][0:HEADS, :]).then_inc(acs_row_done, 1)
            act.wait_ge(acs_row_done, 1)
            act.dma_start(acs_dram, acs_row[:]).then_inc(acs_stored, 16)
            nc.scalar.copy(decay[:, 0, 0:1], eps[:]).then_inc(exps_done, 1)
            for k in range(DT):
                act.wait_ge(x_turned, k + 1)
                nc.scalar.copy(xs[:, k, :], bank[4 + k % 2][:]).then_inc(xs_done, 1)
            act.wait_ge(pads_done, 1)

            def conv_in(page_tile, f):
                unit_ends()
                if f >= 2:
                    act.wait_ge(conv_step, conv.now() + (f - 1) * (SSD_CW - 1))
                u = mm_of(f)
                nc.scalar.copy(pad[:, f % 2, SSD_CW - 1:], u)
                nc.scalar.activation(feat[:, f, :], u, ACT.Identity, bias=one(col_ssd_b(page_tile)),
                                     scale=one(col_ssd_w(SSD_CW - 1, page_tile))).then_inc(evicted, 1)

            def conv_out(f):
                act.wait_ge(conv_step, conv.now() + (f + 1) * (SSD_CW - 1))
                nc.scalar.activation(feat[:, f, :], feat[:, f, :], ACT.Silu).then_inc(silu_done, 1)

            def mm_of(n):
                return bank[n % 2][:]

            seg, bt, st, ymm, yst = Tally(), Tally(), Tally(), Tally(), Tally()
            exps = Tally()
            exps.up()
            with turns(act, 0, GROUPS, per(6) | {conv: 12, seg: 1, bt: 2, st: 2, yst: 8, sq: 2, exps: EXPS}) as g:
                conv_in(CONV_T - 2 * GROUPS + g, 0)
                conv_in(CONV_T - GROUPS + g, 1)
                act.wait_ge(seg_done, seg.up())
                nc.scalar.activation(mask[:], mask[:], ACT.Exp).then_inc(exps_done, 1)
                for j in range(XG):
                    for h in range(HX):
                        rows = slice(h * HD, (h + 1) * HD)
                        nc.scalar.activation(e_row[rows, j, :], acs_b[rows, j * HX + h, P:], ACT.Exp).then_inc(exps_done, 1)
                nc.scalar.activation(decay[:], decay[:], ACT.Exp).then_inc(exps_done, 1)
                nc.scalar.activation(c_decay[:], acs_b[:].rearrange("p h (c l) -> p h c l", l=P)[:, :, 0:C - 1, P - 1],
                                     ACT.Exp).then_inc(exps_done, 1)
                exps.up(EXPS)
                conv_in(g * XG, 2)
                conv_out(0)
                conv_out(1)
                conv_in(g * XG + 1, 3)
                conv_out(2)
                act.wait_ge(cb_turned, bt.up(2))
                nc.scalar.copy(b_tok[:], bank[3][:, 0:LATER]).then_inc(b_tok_done, 1)
                conv_out(3)
                conv.up(4 * (SSD_CW - 1))
                unit_ends()
                nc.scalar.activation(z_act[:, 0, :], bank[0][:], ACT.Silu).then_inc(evicted, 1)
                act.wait_ge(unit_done, units.now() + 1)
                nc.scalar.activation(z_act[:, 1, :], bank[1][:], ACT.Silu).then_inc(evicted, 1)
                act.wait_ge(states_mm, st.up())
                nc.scalar.copy(prev[:, 0, :], bank[6][:, 0:HG * HD]).then_inc(prev0_done, 1)
                st.up()
                unit_ends()
                for j in range(XG):
                    act.wait_ge(y_step, yst.up(4))
                    nc.scalar.activation(y_hi[:, bass.ds(g * XG + j, 1), :], feat[:, 2 + j, :], ACT.Copy,
                                         scale=one(col_norm_w(g * XG + j))).then_inc(y_hi_done, 1)
                    square_of(feat[:, 2 + j, :], j, ahead=0)

            md = Tally()

            def out_proj(o, first):
                for j in range(2):
                    unit_ends()
                    unit_ends()
                    if first and j == 0:
                        root(INNER)
                        keep_row(r_post[:])
                    act.wait_ge(m_done, md.up())
                    square_of(m[:, bass.ds(2 * o + j, 1), :], j)

            out_proj(0, True)
            with turns(act, 1, DT // 2, per(4) | {md: 2, sq: 2}) as o:
                out_proj(o, False)

            def boundary(layer, which):
                root(D)
                with turns(act, 0, DT // 2, {xd: 2, sq: 2}) as i:
                    for n in range(2):
                        k = 2 * i + n
                        act.wait_ge(x_done, xd.up())
                        act.wait_ge(summed, sq.up() - 1)
                        nc.scalar.activation(h_hi[:, bass.ds(k, 1), :], xs[:, bass.ds(k, 1), :], ACT.Copy,
                                             scale=one(col_gain(which, layer, k))).then_inc(h_hi_done, 1)
                        nc.scalar.activation(square[:, n, :], xs[:, bass.ds(k, 1), :], ACT.Square).then_inc(squared, 1)

            def ffn_up(layer, t, first):
                for j in range(2):
                    unit_ends()
                    if first and j == 0:
                        unit_ends()
                        root(D)
                        keep_row(r_pre[:])
                    act.wait_ge(gate_in, gate_n.up())
                    nc.scalar.activation(acc[:], cpad[:, CW - 1:], ACT.Identity, bias=one(col_ffn_b(layer, 2 * t + j)),
                                         scale=one(col_ffn_w(layer, CW - 1, 2 * t + j))).then_inc(acc_done, 1)
                    act.wait_ge(conv_step, conv.up(CW - 1))
                    nc.scalar.activation(acc[:], acc[:], ACT.Silu).then_inc(silu_done, 1)
                    if not (first and j == 0):
                        unit_ends()
                    act.wait_ge(side_step, side.up(2))
                    nc.scalar.activation(hid_hi[:, bass.ds(2 * t + j, 1), :], gated[:], ACT.Copy).then_inc(hid_hi_done, 1)

            def ffn_down(o, last):
                for j in range(2):
                    unit_ends(DOWN[2])
                    unit_ends(0 if last and j else DOWN[0])
                    act.wait_ge(unit_done, units.now() + 1)
                    square_of(bank[4 + j][:], j)
                    nc.scalar.copy(m[:, bass.ds(2 * o + j, 1), :], bank[4 + j][:]).then_inc(m_done, 1)
                    md.up()
                    unit_ends(0 if last and j else DOWN[1])

            for layer in range(DEPTH):
                if layer == 1:
                    boundary(1, MIX_PRE)

                    def sc_in(i, first):
                        for j in range(2):
                            unit_ends()
                            unit_ends()
                            if first and j == 0:
                                root(D)
                                keep_row(r_pre[:])
                            act.wait_ge(gate_in, gate_n.up())
                            nc.scalar.activation(acc[:], cpad[:, CW - 1:], ACT.Copy,
                                                 scale=one(col_sc_w(CW - 1, 2 * i + j))).then_inc(acc_done, 1)
                            unit_ends()
                            conv.up(CW - 1)
                            act.wait_ge(side_step, side.up(3))
                            nc.scalar.activation(hid_hi[:, bass.ds(2 * i + j, 1), :], gated[:], ACT.Copy).then_inc(hid_hi_done, 1)

                    sc_in(0, True)
                    with turns(act, 1, WT // 2, per(6) | {gate_n: 2, conv: 4, side: 6}) as i:
                        sc_in(i, False)
                    with turns(act, 0, DT // 4, per(4) | {md: 4, sq: 4}) as i:
                        for j in range(4):
                            act.wait_ge(unit_done, units.now() + 1)
                            square_of(bank[j][:], j)
                            nc.scalar.copy(m[:, bass.ds(4 * i + j, 1), :], bank[j][:]).then_inc(m_done, 1)
                            md.up()
                            unit_ends()
                boundary(layer, FFN_PRE)
                ffn_up(layer, 0, True)
                with turns(act, 1, FT // 2, per(4) | {gate_n: 2, conv: 4, side: 4}) as t:
                    ffn_up(layer, t, False)
                last_turn = 1 if layer == DEPTH - 1 else 0
                with turns(act, 0, DT // 2 - last_turn, per(6) | {md: 2, sq: 2}) as o:
                    ffn_down(o, False)
                if last_turn:
                    ffn_down(DT // 2 - 1, True)
            root(D)
            for k in range(DT):
                act.wait_ge(out_turned, k + 1)
                nc.scalar.copy(out_tok[:, :, k * P:(k + 1) * P], bank[k % 4][:].rearrange("p (c l) -> p c l", l=P)).then_inc(out_ready, 1)

        @block.vector
        def _(dve):
            lo, units = Tally(), Tally()
            ev, cs, hh, xdn, roots, rows = (Tally() for _ in range(6))
            scaled, mdn = Tally(), Tally()

            def split(kt=KT):
                slot = lo.count % 2
                dve.wait_ge(w_hi_done, lo.up())
                nc.vector.tensor_tensor(w_lo[:, slot, 0:kt, :], w_raw[:, slot, 0:kt, :],
                                        w_hi[:, slot, 0:kt, :].bitcast(F32), ALU.subtract).then_inc(w_lo_done, 1)

            def unit_ends(kt=KT):
                units.up()
                if kt:
                    split(kt)

            def rstd(kept):
                dve.wait_ge(root_done, roots.up())
                nc.vector.reciprocal(rms_tok[:], rms_tok[:]).then_inc(rstd_done, 1)
                if kept:
                    dve.wait_ge(row_done, rows.up())
                else:
                    dve.wait_ge(row_mm, roots.now())

            for c in range(C):
                dve.wait_ge(r_tok_root, c + 1)
                nc.vector.reciprocal(r_tok[:, c:c + 1], r_tok[:, c:c + 1]).then_inc(r_tok_done, 1)
                dve.wait_ge(r_tok_done, c + 1)
                nc.vector.tensor_scalar(xn_tok[:, c, :], x_tok[:, c, :], r_tok[:, c:c + 1], None, ALU.mult).then_inc(xn_ready, 1)
            dve.wait_ge(wdt_split, 1)
            nc.vector.tensor_tensor(wdt_lo[:, :, 0:HEADS], wdt_raw[:], wdt_hi[:, :, 0:HEADS].bitcast(F32), ALU.subtract).then_inc(wdt_split, 1)
            dve.wait_ge(par_done, 1)
            split()
            for k in range(DT):
                dve.wait_ge(h_hi_done, hh.up())
                nc.vector.scalar_tensor_tensor(out=h_lo[:, k, :], in0=bank[2 + k % 4][:], scalar=one(col_gain(MIX_PRE, 0, k)),
                                               in1=h_hi[:, k, :].bitcast(F32), op0=ALU.mult, op1=ALU.subtract).then_inc(h_lo_done, 1)
            split()
            flat = "p (c h) -> p c h"
            dve.wait_ge(dt_mm, 1)
            nc.vector.tensor_tensor(dt_u[:].rearrange(flat, c=C), bank[6][:, 0:C * HEADS].rearrange(flat, c=C),
                                    dt_bias_b[:].unsqueeze(1).to_broadcast([P, C, HEADS]), ALU.add).then_inc(dt_vec, 1)
            dve.wait_ge(dt_act, 4)
            nc.vector.scalar_tensor_tensor(out=dt_tok[:].rearrange("p c h -> p (c h)"), in0=dt_u[:], scalar=0.0, in1=dt_e[:],
                                           op0=ALU.max, op1=ALU.add).then_inc(dt_vec, 1)
            dve.wait_ge(dt_vec, 2)
            nc.vector.scalar_tensor_tensor(out=a_tok[:].rearrange(flat, c=C), in0=dt_tok[:], scalar=-1.0,
                                           in1=a_log_b[:].unsqueeze(1).to_broadcast([P, C, HEADS]),
                                           op0=ALU.mult, op1=ALU.mult).then_inc(dt_vec, 1)
            nc.vector.memset(pad[:, :, 0:SSD_CW - 1], 0.0).then_inc(pads_done, 1)
            dve.wait_ge(small_landed, 64)
            for h in range(HX):
                nc.vector.tensor_copy(d_col[h * HD:(h + 1) * HD, :], d_b[h * HD:(h + 1) * HD, :].rearrange("p (t h) -> p h t", h=HX)[:, h, :])
            dve.wait_ge(acs_mm, 2)
            nc.vector.tensor_copy(acs_tok[:].rearrange("p c h -> p (c h)"), bank[6][:, 0:C * HEADS]).then_inc(acs_tok_done, 1)
            dve.wait_ge(acs_tok_done, 1)
            al, sd, ex, cb, ms, xt, st, p0, ss, ym, ys, yh = (Tally() for _ in range(12))
            ex.up()
            sd.up()

            def conv(f, page_tile):
                if f >= 2:
                    unit_ends()
                dve.wait_ge(evicted, ev.up())
                for tap in range(SSD_CW - 1):
                    if tap:
                        dve.wait_ge(conv_step, cs.now())
                    nc.vector.scalar_tensor_tensor(out=feat[:, f, :], in0=pad[:, f % 2, tap:tap + T],
                                                   scalar=one(col_ssd_w(tap, page_tile)), in1=feat[:, f, :],
                                                   op0=ALU.mult, op1=ALU.add).then_inc(conv_step, 1)
                    cs.up()

            def by_head(ap):
                return ap.rearrange("p (h e) -> p h e", e=HD)

            with turns(dve, 0, GROUPS, {lo: 6, units: 6, ev: 6, cs: 12, al: 1, sd: 1, ex: EXPS, cb: 1, ms: 2, xt: 2,
                                        st: 2, p0: 1, ss: 4, ym: 2, ys: 8, yh: 2}) as g:
                unit_ends()
                dve.wait_ge(acs_landed, 16 * al.up())
                nc.vector.tensor_tensor(decay[:], acs_b[:].rearrange("p h (c l) -> p h c l", l=P)[:, :, 0:C - 1, P - 1],
                                        acs_tok[:, 0:C - 1, bass.ds(g * HG, HG)].rearrange("p c h -> p h c"), ALU.subtract)
                dve.wait_ge(scan_done, sd.now())
                sd.up()
                for h in range(HG):
                    for c in range(C):
                        span = slice(c * P, (c + 1) * P)
                        last = nc.vector.tensor_scalar(mask[:, h, span], acs_b[:, h, span], acs_tok[:, c, bass.ds(g * HG + h, 1)],
                                                       0.0, ALU.subtract, ALU.min)
                last.then_inc(seg_done, 1)
                unit_ends()
                conv(0, CONV_T - 2 * GROUPS + g)
                conv(1, CONV_T - GROUPS + g)
                conv(2, g * XG)
                conv(3, g * XG + 1)
                dve.wait_ge(cb_turned, cb.now() * 2 + 1)
                cb.up()
                nc.vector.tensor_tensor(cbm[:].rearrange("p (c l) -> p c l", l=P), bank[2][:].rearrange("p (c l) -> p c l", l=P),
                                        tri[:].unsqueeze(1).to_broadcast([P, C, P]), ALU.mult).then_inc(mask_step, 1)
                dve.wait_ge(mask_step, ms.up())
                dve.wait_ge(exps_done, ex.up(EXPS))
                nc.vector.tensor_tensor(mask[:], mask[:], cbm[:].unsqueeze(1).to_broadcast([P, HG, T]), ALU.mult).then_inc(mask_step, 1)
                ms.up()
                unit_ends()
                for j in range(XG):
                    dve.wait_ge(x_tok_turned, xt.up())
                    nc.vector.tensor_tensor(
                        xdt[:, :, j * P:(j + 1) * P].rearrange("p c (h e) -> p c h e", e=HD),
                        bank[4 + j][:].rearrange("p (c h e) -> p c h e", c=C, e=HD),
                        dt_tok[:, :, bass.ds(g * HG + j * HX, HX)].unsqueeze(3).to_broadcast([P, C, HX, HD]),
                        ALU.mult).then_inc(xdt_done, 1)
                dve.wait_ge(xdt_done, (xt.now() // 2) * 3 - 1 if xt.i is None else xt.i * 3 + 2)
                nc.vector.tensor_tensor(
                    xdd[:].rearrange("p c (h e) -> p c h e", e=HD),
                    xdt[:, 0:C - 1, :].rearrange("p c (h e) -> p c h e", e=HD),
                    decay[:].rearrange("p h c -> p c h").unsqueeze(3).to_broadcast([P, C - 1, HG, HD]),
                    ALU.mult).then_inc(xdt_done, 1)
                dve.wait_ge(states_mm, st.up(2))
                dve.wait_ge(prev0_done, p0.up())
                for c in range(1, C - 1):
                    if c > 1:
                        dve.wait_ge(state_step, ss.now())
                    nc.vector.tensor_tensor(by_head(prev[:, c, :]), by_head(prev[:, c - 1, :]),
                                            c_decay[:, :, c:c + 1].to_broadcast([P, HG, HD]), ALU.mult).then_inc(state_step, 1)
                    dve.wait_ge(state_step, ss.up())
                    nc.vector.tensor_tensor(prev[:, c, :], prev[:, c, :],
                                            bank[6 + c // 2][:, c % 2 * HG * HD:(c % 2 + 1) * HG * HD], ALU.add).then_inc(state_step, 1)
                    ss.up()
                unit_ends()
                dve.wait_ge(evicted, ev.up(2))
                for j in range(XG):
                    dve.wait_ge(y_mm, ym.up())
                    nc.vector.tensor_tensor(e_row[:, j, :], e_row[:, j, :], bank[2 + j][:, P:], ALU.mult).then_inc(y_step, 1)
                    nc.vector.scalar_tensor_tensor(out=feat[:, 2 + j, :], in0=feat[:, 2 + j, :],
                                                   scalar=d_col[:, bass.ds(g * XG + j, 1)], in1=bank[4 + j][:],
                                                   op0=ALU.mult, op1=ALU.add).then_inc(y_step, 1)
                    dve.wait_ge(y_step, ys.up(2))
                    nc.vector.tensor_tensor(feat[:, 2 + j, P:], feat[:, 2 + j, P:], e_row[:, j, :], ALU.add).then_inc(y_step, 1)
                    dve.wait_ge(y_step, ys.up())
                    nc.vector.tensor_tensor(feat[:, 2 + j, :], feat[:, 2 + j, :], z_act[:, j, :], ALU.mult).then_inc(y_step, 1)
                    ys.up()
                for j in range(XG):
                    dve.wait_ge(y_hi_done, yh.up())
                    nc.vector.scalar_tensor_tensor(out=y_lo[:, bass.ds(g * XG + j, 1), :], in0=feat[:, 2 + j:3 + j, :],
                                                   scalar=one(col_norm_w(g * XG + j)), in1=y_hi[:, bass.ds(g * XG + j, 1), :].bitcast(F32),
                                                   op0=ALU.mult, op1=ALU.subtract).then_inc(y_lo_done, 1)

            def out_proj(o, first):
                for j in range(2):
                    unit_ends()
                    if first and j == 0:
                        unit_ends()
                        rstd(True)
                    dve.wait_ge(unit_done, units.now() + (0 if first and j == 0 else 1))
                    nc.vector.tensor_tensor(m[:, bass.ds(2 * o + j, 1), :], bank[j][:].unsqueeze(1), r_post[:].unsqueeze(1),
                                            ALU.mult).then_inc(m_done, 1)
                    mdn.up()
                    if not (first and j == 0):
                        unit_ends()

            out_proj(0, True)
            with turns(dve, 1, DT // 2, {lo: 4, units: 4, mdn: 2}) as o:
                out_proj(o, False)

            def scale(i):
                nc.vector.tensor_tensor(side[:], m[:, bass.ds(2 * i, 2), :], bank[7][:].unsqueeze(1).to_broadcast([P, 2, T]),
                                        ALU.mult).then_inc(scaled_done, 1)

            def residual(i, layer, which):
                dve.wait_ge(scaled_done, scaled.up())
                for n in range(2):
                    nc.vector.scalar_tensor_tensor(out=xs[:, bass.ds(2 * i + n, 1), :], in0=side[:, n:n + 1, :],
                                                   scalar=one(col_gain(which, layer, 2 * i + n)), in1=xs[:, bass.ds(2 * i + n, 1), :],
                                                   op0=ALU.mult, op1=ALU.add).then_inc(x_done, 1)
                    xdn.up()

            def low(i, layer, which):
                for n in range(2):
                    dve.wait_ge(h_hi_done, hh.up())
                    nc.vector.scalar_tensor_tensor(out=h_lo[:, bass.ds(2 * i + n, 1), :], in0=xs[:, bass.ds(2 * i + n, 1), :],
                                                   scalar=one(col_gain(which, layer, 2 * i + n)),
                                                   in1=h_hi[:, bass.ds(2 * i + n, 1), :].bitcast(F32),
                                                   op0=ALU.mult, op1=ALU.subtract).then_inc(h_lo_done, 1)

            def boundary(post, pre):
                rstd(False)
                dve.wait_ge(m_done, mdn.now())
                scale(0)
                with turns(dve, 0, DT // 2 - 1, {scaled: 1, xdn: 2} | ({hh: 2} if pre else {})) as i:
                    residual(i, *post)
                    dve.wait_ge(x_done, xdn.now())
                    scale(i + 1)
                    if pre:
                        low(i, *pre)
                residual(DT // 2 - 1, *post)
                if pre:
                    low(DT // 2 - 1, *pre)

            hd, ac, sl, st2 = Tally(), Tally(), Tally(), Tally()
            sl.up(4 * GROUPS)

            def conv_taps(cols):
                dve.wait_ge(acc_done, ac.up())
                for tap in range(CW - 1):
                    if tap:
                        dve.wait_ge(conv_step, cs.now())
                    nc.vector.scalar_tensor_tensor(out=acc[:], in0=cpad[:, tap:tap + T], scalar=one(cols(tap)), in1=acc[:],
                                                   op0=ALU.mult, op1=ALU.add).then_inc(conv_step, 1)
                    cs.up()

            def low_hidden(t):
                dve.wait_ge(hid_hi_done, hd.up())
                nc.vector.tensor_tensor(hid_lo[:, bass.ds(t, 1), :], gated[:].unsqueeze(1), hid_hi[:, bass.ds(t, 1), :].bitcast(F32),
                                        ALU.subtract).then_inc(hid_lo_done, 1)

            def ffn_up(layer, t, first):
                for j in range(2):
                    unit_ends()
                    if first and j == 0:
                        unit_ends()
                        rstd(True)
                    dve.wait_ge(unit_done, units.now())
                    nc.vector.tensor_tensor(cpad[:, CW - 1:], bank[2 * j][:], r_pre[:], ALU.mult).then_inc(gate_in, 1)
                    conv_taps(lambda tap: col_ffn_w(layer, tap, 2 * t + j))
                    if not (first and j == 0):
                        unit_ends()
                    dve.wait_ge(unit_done, units.now())
                    nc.vector.tensor_tensor(side[:, 0, :], bank[2 * j + 1][:], r_pre[:], ALU.mult).then_inc(side_step, 1)
                    dve.wait_ge(side_step, st2.up())
                    dve.wait_ge(silu_done, sl.up())
                    nc.vector.tensor_tensor(gated[:], side[:, 0, :], acc[:], ALU.mult).then_inc(side_step, 1)
                    st2.up()
                    low_hidden(2 * t + j)

            def sc_in(i, first):
                for j in range(2):
                    unit_ends()
                    if first and j == 0:
                        unit_ends()
                        rstd(True)
                        nc.vector.tensor_tensor(r_pre2[:], r_pre[:], r_pre[:], ALU.mult).then_inc(pre2_done, 1)
                        dve.wait_ge(pre2_done, 1)
                    dve.wait_ge(unit_done, units.now())
                    nc.vector.tensor_tensor(side[:, 0, :], bank[3 * j][:], r_pre2[:], ALU.mult).then_inc(side_step, 1)
                    dve.wait_ge(side_step, st2.up())
                    if not (first and j == 0):
                        unit_ends()
                    dve.wait_ge(unit_done, units.now())
                    nc.vector.tensor_tensor(cpad[:, CW - 1:], side[:, 0, :], bank[3 * j + 1][:], ALU.mult).then_inc(gate_in, 1)
                    conv_taps(lambda tap: col_sc_w(tap, 2 * i + j))
                    unit_ends()
                    dve.wait_ge(unit_done, units.now())
                    nc.vector.tensor_tensor(side[:, 0, :], bank[3 * j + 2][:], r_pre[:], ALU.mult).then_inc(side_step, 1)
                    dve.wait_ge(side_step, st2.up())
                    dve.wait_ge(conv_step, cs.now())
                    nc.vector.tensor_tensor(gated[:], side[:, 0, :], acc[:], ALU.mult).then_inc(side_step, 1)
                    st2.up()
                    low_hidden(2 * i + j)

            for layer in range(DEPTH):
                if layer == 1:
                    boundary((0, FFN_POST), (1, MIX_PRE))
                    sc_in(0, True)
                    with turns(dve, 1, WT // 2, {lo: 6, units: 6, cs: 4, ac: 2, hd: 2, st2: 6}) as i:
                        sc_in(i, False)
                    with turns(dve, 0, DT // 4, {lo: 4, units: 4}):
                        for j in range(4):
                            unit_ends()
                    mdn.up(DT)
                else:
                    nc.vector.memset(cpad[:, 0:CW - 1], 0.0).then_inc(pads_done, 1)
                    dve.wait_ge(pads_done, 2)
                boundary((layer, MIX_POST), (layer, FFN_PRE))
                ffn_up(layer, 0, True)
                with turns(dve, 1, FT // 2, {lo: 4, units: 4, cs: 4, ac: 2, hd: 2, st2: 4, sl: 2}) as t:
                    ffn_up(layer, t, False)
                last_turn = 1 if layer == DEPTH - 1 else 0
                with turns(dve, 0, DT // 2 - last_turn, {lo: 6, units: 6}):
                    for n in range(6):
                        unit_ends(DOWN[(n + 2) % 3])
                if last_turn:
                    for n in range(6):
                        unit_ends(DOWN[(n + 2) % 3] if n < 4 else 0)
                mdn.up(DT)
            boundary((1, FFN_POST), None)

        @block.tensor
        def _(pe):
            lo, sm, sqs, hl, rs = (Tally() for _ in range(5))

            def three(dst, wh, wl, xh, xl, start, stop):
                nc.tensor.matmul(dst, wh, xh, start=start, stop=False)
                nc.tensor.matmul(dst, wl, xh, start=False, stop=False)
                return nc.tensor.matmul(dst, wh, xl, start=False, stop=stop)

            def unit(dst, in_hi, in_lo, kt=KT, k0=0, start=True, stop=True, by_tile=None):
                slot = lo.count % 2
                pe.wait_ge(w_lo_done, lo.up())
                for k in range(kt):
                    if by_tile:
                        pe.wait_ge(by_tile[0], by_tile[1] + k + 1)
                    last = three(dst, w_hi[:, slot, k, :], w_lo[:, slot, k, :], in_hi[:, k0 + k, :], in_lo[:, k0 + k, :],
                                 start and k == 0, stop and k == kt - 1)
                last.then_inc(unit_done, 1)

            def two_units(dst0, dst1):
                pe.wait_ge(w_lo_done, lo.up(2))
                for k in range(KT):
                    pe.wait_ge(h_lo_done, hl.up())
                    for slot, dst in enumerate((dst0, dst1)):
                        last = three(dst, w_hi[:, slot, k, :], w_lo[:, slot, k, :], h_hi[:, k, :], h_lo[:, k, :], k == 0, k == KT - 1)
                        if k == KT - 1:
                            last.then_inc(unit_done, 1)

            def norm_sum(tiles):
                pe.wait_ge(summed, sm.up(tiles))
                pe.wait_ge(squared, sqs.up(tiles))
                for c in range(C):
                    span = slice(c * P, (c + 1) * P)
                    nc.tensor.matmul(bank[6][:, c:c + 1], total[:, span], ones[:, 0:1], start=True, stop=False)
                    last = nc.tensor.matmul(bank[6][:, c:c + 1], square[:, 1, span], ones[:, 0:1], start=False, stop=True)
                last.then_inc(norm_mm, 1)

            def norm_row():
                pe.wait_ge(rstd_done, rs.up())
                for c in range(C):
                    last = nc.tensor.transpose(bank[7][:, c * P:(c + 1) * P], rms_tok[:, c:c + 1].to_broadcast([P, P]), ident[:])
                last.then_inc(row_mm, 1)

            pe.wait_ge(consts_done, 4)
            pe.wait_ge(params_landed, 16 * N_PARAM)
            for n in range(4):
                last = nc.tensor.transpose(bank[6][:, n * P:n * P + ROWS[n]], pages[0:ROWS[n], n, :], ident[0:ROWS[n], 0:ROWS[n]])
            last.then_inc(pages_turned, 1)
            pe.wait_ge(xn_ready, C)
            for k in range(DT):
                if k >= 4:
                    pe.wait_ge(h_lo_done, k - 3)
                for c in range(C):
                    last = nc.tensor.transpose(bank[2 + k % 4][:, c * P:(c + 1) * P], xn_tok[:, c, k * P:(k + 1) * P], ident[:])
                last.then_inc(xn_done, 1)
            ev, si, bt, mk, xd, ss = (Tally() for _ in range(6))

            def group_unit(n):
                ev.up()
                if ev.i is not None or ev.now() > 2:
                    pe.wait_ge(evicted, ev.now() - 2)
                unit(bank[n % 2][:], h_hi, h_lo)

            pe.wait_ge(par_done, 1)
            pe.wait_ge(wdt_split, 2)
            pe.wait_ge(h_lo_done, hl.up(DT))
            for k in range(DT):
                last = three(bank[7][:], wdt_hi[:, k, :], wdt_lo[:, k, :], h_hi[:, k, :], h_lo[:, k, :], k == 0, k == DT - 1)
            last.then_inc(dt_row_mm, 1)
            pe.wait_ge(dt_row_done, 1)
            for c in range(C):
                last = nc.tensor.transpose(bank[6][:, c * HEADS:(c + 1) * HEADS], dt_row[:, c * P:(c + 1) * P], ident[0:HEADS, 0:HEADS])
            last.then_inc(dt_mm, 1)
            group_unit(0)
            pe.wait_ge(dt_vec, 3)
            for c in range(C):
                last = nc.tensor.matmul(bank[7][0:HEADS, c * P:(c + 1) * P], a_tok[:, c * HEADS:(c + 1) * HEADS], tri[:],
                                        start=True, stop=True)
            last.then_inc(acs_mm, 1)
            nc.tensor.matmul(bank[6][:, 0:C * HEADS], tri[:], a_tok[:], start=True, stop=True).then_inc(acs_mm, 1)
            group_unit(1)
            for k in range(DT):
                if k >= 2:
                    pe.wait_ge(xs_done, k - 1)
                for c in range(C):
                    last = nc.tensor.transpose(bank[4 + k % 2][:, c * P:(c + 1) * P], x_tok[:, c, k * P:(k + 1) * P], ident[:])
                last.then_inc(x_turned, 1)
            pe.wait_ge(acs_row_done, 1)
            nc.tensor.transpose(bank[7][:, 0:P], ident[:], ident[:]).then_inc(scan_done, 1)

            def group(last_group):
                group_unit(2)
                group_unit(3)
                pe.wait_ge(silu_done, si.up(2))
                for c in range(C):
                    span = slice(c * P, (c + 1) * P)
                    last = nc.tensor.matmul(bank[2][:, span], feat[:, 0, span], feat[:, 1, span], start=True, stop=True)
                last.then_inc(cb_turned, 1)
                for c in range(C - 1):
                    last = nc.tensor.transpose(bank[3][:, c * P:(c + 1) * P], feat[:, 0, c * P:(c + 1) * P], ident[:])
                last.then_inc(cb_turned, 1)
                group_unit(4)
                for j in range(XG):
                    pe.wait_ge(silu_done, si.up())
                    for c in range(C):
                        last = nc.tensor.transpose(bank[4 + j][:, c * P:(c + 1) * P], feat[:, 2 + j, c * P:(c + 1) * P], ident[:])
                    last.then_inc(x_tok_turned, 1)
                group_unit(5)
                pe.wait_ge(b_tok_done, bt.up())
                pe.wait_ge(xdt_done, xd.up(3))
                for c in range(C - 1):
                    last = nc.tensor.matmul(bank[6 + c // 2][:, c % 2 * HG * HD:(c % 2 + 1) * HG * HD], b_tok[:, c * P:(c + 1) * P],
                                            xdd[:, c, :], start=True, stop=True)
                    if c:
                        last.then_inc(states_mm, 1)
                pe.wait_ge(mask_step, mk.up(2))
                for j in range(XG):
                    for h in range(HX):
                        for c in range(C):
                            cols = slice(j * P + h * HD, j * P + (h + 1) * HD)
                            last = nc.tensor.matmul(bank[4 + j][h * HD:(h + 1) * HD, c * P:(c + 1) * P], xdt[:, c, cols],
                                                    mask[:, j * HX + h, c * P:(c + 1) * P], start=True, stop=True)
                last.then_inc(scan_done, 1)
                pe.wait_ge(prev0_done, bt.now())
                pe.wait_ge(state_step, ss.up(4))
                for j in range(XG):
                    for c in range(1, C):
                        last = nc.tensor.matmul(bank[2 + j][:, c * P:(c + 1) * P], prev[:, c - 1, j * P:(j + 1) * P],
                                                feat[:, 1, c * P:(c + 1) * P], start=True, stop=True)
                    last.then_inc(y_mm, 1)
                if not last_group:
                    group_unit(0)
                    group_unit(1)

            with turns(pe, 0, GROUPS - 1, {lo: 6, ev: 6, si: 4, bt: 1, mk: 2, xd: 3, ss: 4}):
                group(False)
            group(True)

            def out_proj(first):
                for j in range(2):
                    if first and j == 0:
                        pe.wait_ge(y_lo_done, KT)
                    unit(bank[j][:], y_hi, y_lo, stop=False)
                    if first and j == 0:
                        pe.wait_ge(y_lo_done, IT)
                    if first and j == 1:
                        norm_row()
                    unit(bank[j][:], y_hi, y_lo, k0=KT, start=False)
                    if first and j == 0:
                        norm_sum(IT)

            pe.wait_ge(evicted, ev.now())
            out_proj(True)
            with turns(pe, 1, DT // 2, {lo: 4}):
                out_proj(False)

            def up_proj(banks, first):
                if first:
                    two_units(bank[0][:], bank[1][:])
                    norm_sum(DT)
                    unit(bank[2][:], h_hi, h_lo)
                    norm_row()
                for n in range(3 if first else 0, banks):
                    unit(bank[n][:], h_hi, h_lo)

            def down_proj(first):
                for j in range(2):
                    for n, kt in enumerate(DOWN):
                        if first and j == 0:
                            pe.wait_ge(hid_lo_done, hidden - FT + n * KT + kt)
                        unit(bank[4 + j][:], hid_hi, hid_lo, kt=kt, k0=n * KT, start=n == 0, stop=n == 2)

            hidden = 0
            for layer in range(DEPTH):
                norm_sum(DT)
                norm_row()
                if layer == 1:
                    up_proj(6, True)
                    with turns(pe, 1, WT // 2, {lo: 6}):
                        up_proj(6, False)
                    for n in range(4):
                        unit(bank[n][:], hid_hi, hid_lo, by_tile=None if n else (hid_lo_done, hidden))
                    with turns(pe, 1, DT // 4, {lo: 4}):
                        for n in range(4):
                            unit(bank[n][:], hid_hi, hid_lo)
                    hidden += WT
                    norm_sum(DT)
                    norm_row()
                up_proj(4, True)
                with turns(pe, 1, FT // 2, {lo: 4}):
                    up_proj(4, False)
                hidden += FT
                down_proj(True)
                with turns(pe, 1, DT // 2, {lo: 6}):
                    down_proj(False)
            norm_sum(DT)
            norm_row()
            for k in range(DT):
                pe.wait_ge(x_done, 3 * DT + k + 1)
                if k >= 4:
                    pe.wait_ge(out_ready, k - 3)
                for c in range(C):
                    last = nc.tensor.transpose(bank[k % 4][:, c * P:(c + 1) * P], xs[:, k, c * P:(c + 1) * P], ident[:])
                last.then_inc(out_turned, 1)


_INS = ["x", "mix_pre_g", "mix_post_g", "ffn_pre_g", "ffn_post_g", "ssd_w_in", "ssd_conv_w", "ssd_conv_b", "ssd_dt_bias",
        "ssd_A_log", "ssd_D", "ssd_norm_w", "ssd_w_out", "sc_w_in", "sc_conv_w", "sc_w_out", "ffn_w_up", "ffn_conv_w",
        "ffn_conv_b", "ffn_w_down"]


def kernel(**inputs):
    import numpy as np
    import concourse.bacc as bacc
    from concourse.bass_utils import run_bass_kernel_spmd

    nc = bacc.Bacc("TRN2", target_bir_lowering=False, num_devices=1)
    arrays, args = {}, []
    for name in _INS:
        a = np.ascontiguousarray(inputs[name])
        arrays[f"in_{name}"] = a
        args.append(nc.dram_tensor(f"in_{name}", a.shape, mybir.dt.from_np(a.dtype), kind="ExternalInput").ap())
    args.append(nc.dram_tensor("out_0", inputs["x"].shape, F32, kind="ExternalOutput").ap())
    build(nc, *args)
    r = run_bass_kernel_spmd(nc, [arrays], core_ids=[0])
    return r.results[0]["out_0"]
```

```python
from contextlib import ExitStack, contextmanager
from functools import partial

import concourse.bass as bass
from concourse import mybir

F32 = mybir.dt.float32
F32R = mybir.dt.float32r
ALU = mybir.AluOpType
ACT = mybir.ActivationFunctionType

P = 128
EPS = 1e-6
KT = 8
HALF = KT // 2


class Tally:

    def __init__(self):
        self.start, self.count, self.per, self.i = 0, 0, 0, None

    def now(self):
        n = self.start + self.count
        return n if self.i is None else self.i * self.per + n

    def up(self, n=1):
        self.count += n
        return self.now()


@contextmanager
def turns(engine, first, end, per):
    for t in per:
        t.start, t.count = t.start + t.count - first * per[t], 0
    with engine.Fori(first, end) as i:
        for t, n in per.items():
            t.i, t.per = i, n
        yield i
        for n, t in enumerate(per):
            assert t.count == t.per, (n, t.count, t.per)
    for t in per:
        t.start, t.count, t.i = t.start + end * t.per, 0, None


def build(nc, x, mix_pre_g, mix_post_g, ffn_pre_g, ffn_post_g, ssd_w_in, ssd_conv_w, ssd_conv_b,
          ssd_dt_bias, ssd_A_log, ssd_D, ssd_norm_w, ssd_w_out, sc_w_in, sc_conv_w, sc_w_out,
          ffn_w_up, ffn_conv_w, ffn_conv_b, ffn_w_down, out):
    _, T, D = x.shape
    C = T // P
    DT = D // P
    DEPTH = mix_pre_g.shape[0]
    INNER = ssd_norm_w.shape[1]
    IT = INNER // P
    HEADS = ssd_D.shape[1]
    GROUPS = 8
    HG = HEADS // GROUPS
    XG = IT // GROUPS
    HX = HG // XG
    HD = P // HX
    STATE = P
    SSD_CW = ssd_conv_w.shape[1]
    CONV_T = ssd_conv_w.shape[2] // P
    W = sc_conv_w.shape[2]
    WT = W // P
    HIDDEN = ffn_conv_b.shape[1]
    FT = HIDDEN // P
    CW = ffn_conv_w.shape[1]
    DOWN = [KT, KT, FT - 2 * KT]
    HERE, HERE_LAST = 2, 4
    LATER = T - P
    EXPS = 3 + XG * HX
    assert (T, D, C, DT, DEPTH, IT, FT, HD, CW, SSD_CW) == (512, 1024, 4, 8, 2, 16, 22, 64, 3, 4)

    def col_ssd_w(tap, t):
        return 0, tap * CONV_T + t

    def col_ssd_b(t):
        return 1, t

    GAINS = CONV_T

    def col_gain(which, layer, k):
        return 1, GAINS + which * DEPTH * DT + layer * DT + k

    NORM_W = GAINS + 4 * DEPTH * DT
    MIX_PRE, MIX_POST, FFN_PRE, FFN_POST = range(4)

    def col_norm_w(t):
        return 1, NORM_W + t

    def col_ffn_w(layer, tap, t):
        return 2 + layer, tap * FT + t

    def col_ffn_b(layer, t):
        return 2, CW * FT + layer * FT + t

    def col_sc_w(tap, t):
        return 3, CW * FT + tap * WT + t

    PAGES = [
        [(0, ssd_conv_w[0].rearrange("k (t p) -> (k t) p", p=P))],
        [(0, ssd_conv_b[0].rearrange("(t p) -> t p", p=P))]
        + [(GAINS + n * DEPTH * DT, g.rearrange("l (k p) -> (l k) p", p=P))
           for n, g in enumerate((mix_pre_g, mix_post_g, ffn_pre_g, ffn_post_g))]
        + [(NORM_W, ssd_norm_w[0].rearrange("(t p) -> t p", p=P))],
        [(0, ffn_conv_w[0].rearrange("k (t p) -> (k t) p", p=P)),
         (CW * FT, ffn_conv_b.rearrange("l (t p) -> (l t) p", p=P))],
        [(0, ffn_conv_w[1].rearrange("k (t p) -> (k t) p", p=P)),
         (CW * FT, sc_conv_w[0].rearrange("k (t p) -> (k t) p", p=P))],
    ]
    ROWS = [max(at + s.shape[0] for at, s in page) for page in PAGES]
    N_PARAM = sum(len(page) for page in PAGES)

    w_in = ssd_w_in[0].rearrange("(k p) n -> p k n", p=P)
    w_out = ssd_w_out[0].rearrange("(k p) n -> p k n", p=P)
    w_sc = sc_w_in[0].rearrange("(k p) n -> p k n", p=P)
    w_sc_out = sc_w_out[0].rearrange("(k p) n -> p k n", p=P)
    w_up = [ffn_w_up[l].rearrange("(k p) n -> p k n", p=P) for l in range(DEPTH)]
    w_down = [ffn_w_down[l].rearrange("(k p) n -> p k n", p=P) for l in range(DEPTH)]
    AT_X, AT_B = INNER, 2 * INNER
    AT_C = AT_B + GROUPS * STATE
    AT_DT = AT_C + GROUPS * STATE

    acs_dram = nc.dram_tensor("acs_dram", [HEADS, T], F32, kind="Internal").ap()

    ctx = ExitStack()
    with ctx:
        def sb(name, shape, dt=F32, stack=ctx):
            return stack.enter_context(nc.sbuf_tensor(name, shape, dt))

        def sem(name):
            return ctx.enter_context(nc.semaphore(name))

        bank = [ctx.enter_context(nc.psum_tensor(f"bank{n}", [P, 512], F32)) for n in range(8)]

        xs = sb("xs", [P, DT, T])
        h_hi, h_lo = sb("h_hi", [P, DT, T], F32R), sb("h_lo", [P, DT, T], F32R)
        w_raw = sb("w_raw", [P, 2, KT, P])
        w_hi, w_lo = sb("w_hi", [P, 2, KT, P], F32R), sb("w_lo", [P, 2, KT, P], F32R)
        ident, ones, tri = sb("ident", [P, P]), sb("ones", [P, P]), sb("tri", [P, P])
        par = sb("par", [P, 4, P])
        eps, unread = sb("eps", [P, 1]), sb("unread", [P, 1 + DEPTH])
        r_post, r_pre, r_pre2 = sb("r_post", [P, T]), sb("r_pre", [P, T]), sb("r_pre2", [P, T])
        square, total = sb("square", [P, 2, T]), sb("total", [P, T])
        rms_tok = sb("rms_tok", [P, C])

        with ExitStack() as start:
            x_tok = sb("x_tok", [P, C, D], stack=start)
            xn_tok = sb("xn_tok", [P, C, D], stack=start)
            pages = sb("pages", [P, 4, P], stack=start)
        with ExitStack() as ssd:
            y_hi, y_lo = sb("y_hi", [P, IT, T], F32R, ssd), sb("y_lo", [P, IT, T], F32R, ssd)
            acs_tok, dt_tok = sb("acs_tok", [P, C, HEADS], stack=ssd), sb("dt_tok", [P, C, HEADS], stack=ssd)
            d_col = sb("d_col", [P, IT], stack=ssd)
            acs_b = sb("acs_b", [P, HG, T], stack=ssd)
            mask = sb("mask", [P, HG, T], stack=ssd)
            feat = sb("feat", [P, 4, T], stack=ssd)
            pad = sb("pad", [P, 2, SSD_CW - 1 + T], stack=ssd)
            cbm = sb("cbm", [P, T], stack=ssd)
            b_tok = sb("b_tok", [P, LATER], stack=ssd)
            xdt = sb("xdt", [P, C, HG * HD], stack=ssd)
            xdd = sb("xdd", [P, C - 1, HG * HD], stack=ssd)
            prev = sb("prev", [P, C - 1, HG * HD], stack=ssd)
            e_row = sb("e_row", [P, XG, LATER], stack=ssd)
            z_act = sb("z_act", [P, XG, T], stack=ssd)
            decay, c_decay = sb("decay", [P, HG, C - 1], stack=ssd), sb("c_decay", [P, HG, C - 1], stack=ssd)
        with ExitStack() as small:
            sb("under", [P, 2 * IT * T + 2 * C * HEADS + IT], stack=small)
            wdt_raw = sb("wdt_raw", [P, DT, HEADS], stack=small)
            wdt_hi, wdt_lo = sb("wdt_hi", [P, DT, P], F32R, small), sb("wdt_lo", [P, DT, P], F32R, small)
            dt_row = sb("dt_row", [HEADS, T], stack=small)
            a_log_b, dt_bias_b, d_b = (sb(n, [P, HEADS], stack=small) for n in ("a_log_b", "dt_bias_b", "d_b"))
            sum_sq, r_tok = sb("sum_sq", [P, C], stack=small), sb("r_tok", [P, C], stack=small)
            dt_u, dt_e, a_tok = (sb(n, [P, C * HEADS], stack=small) for n in ("dt_u", "dt_e", "a_tok"))
            acs_row = sb("acs_row", [HEADS, T], stack=small)
        with ExitStack() as rest:
            hid_hi, hid_lo = sb("hid_hi", [P, FT, T], F32R, rest), sb("hid_lo", [P, FT, T], F32R, rest)
            m = sb("m", [P, DT, T], stack=rest)
            cpad = sb("cpad", [P, CW - 1 + T], stack=rest)
            acc, gated, side = sb("acc", [P, T], stack=rest), sb("gated", [P, T], stack=rest), sb("side", [P, 2, T], stack=rest)
        with ExitStack() as end:
            out_tok = sb("out_tok", [P, C, D], stack=end)
        with ExitStack() as between:
            squares = sb("squares", [P, DT, T], stack=between)

        x_landed = [sem(f"x_landed{c}") for c in range(C)]
        params_landed, small_landed = sem("params_landed"), sem("small_landed")
        raw_landed = [sem("raw_landed0"), sem("raw_landed1")]
        acs_stored, acs_landed, out_stored = sem("acs_stored"), sem("acs_landed"), sem("out_stored")
        w_hi_done, w_lo_done, unit_done = sem("w_hi_done"), sem("w_lo_done"), sem("unit_done")
        half_unit_done, half_hi_done, half_lo_done = sem("half_unit_done"), sem("half_hi_done"), sem("half_lo_done")
        consts_done, x_squared, r_tok_root, r_tok_done = (sem(n) for n in ("consts_done", "x_squared", "r_tok_root", "r_tok_done"))
        xn_ready = sem("xn_ready")
        xn_done, x_turned, pages_turned, par_done = (sem(n) for n in ("xn_done", "x_turned", "pages_turned", "par_done"))
        wdt_cleared, dt_row_mm, dt_row_done = sem("wdt_cleared"), sem("dt_row_mm"), sem("dt_row_done")
        dt_mm, dt_act, dt_vec, acs_mm, acs_row_done, acs_tok_done, wdt_split = (
            sem(n) for n in ("dt_mm", "dt_act", "dt_vec", "acs_mm", "acs_row_done", "acs_tok_done", "wdt_split"))
        h_hi_done, h_lo_done, evicted, pads_done = (sem(n) for n in ("h_hi_done", "h_lo_done", "evicted", "pads_done"))
        xs_done = [sem("xs_done_even"), sem("xs_done_odd")]
        seg_done, exps_done, conv_step, silu_done = sem("seg_done"), sem("exps_done"), sem("conv_step"), sem("silu_done")
        cb_turned, b_tok_done, mask_step = sem("cb_turned"), sem("b_tok_done"), sem("mask_step")
        x_tok_turned, xdt_done, states_mm, prev0_done, state_step = (
            sem(n) for n in ("x_tok_turned", "xdt_done", "states_mm", "prev0_done", "state_step"))
        y_mm, y_step, y_hi_done, y_lo_done, scan_done = (sem(n) for n in ("y_mm", "y_step", "y_hi_done", "y_lo_done", "scan_done"))
        squared, summed, norm_mm, root_done, rstd_done, row_mm, row_done, pre2_done = (
            sem(n) for n in ("squared", "summed", "norm_mm", "root_done", "rstd_done", "row_mm", "row_done", "pre2_done"))
        m_done, scaled_done, upper_scaled, x_done = (sem(n) for n in ("m_done", "scaled_done", "upper_scaled", "x_done"))
        gate_in, acc_done, side_step, hid_hi_done, hid_lo_done = (
            sem(n) for n in ("gate_in", "acc_done", "side_step", "hid_hi_done", "hid_lo_done"))
        out_turned, out_ready = sem("out_turned"), sem("out_ready")

        def one(page_col):
            return par[:, page_col[0], bass.ds(page_col[1], 1)]

        GROUP_BANKS = (6, 7, 0, 1, 0, 1)
        PE_SUMS = 2
        LAG = 2
        WARM = 4, 3, 12, 8
        WARM_OUT = 3, 6
        SUM_AT, ROW_AT = 2, 5
        block = ctx.enter_context(nc.Block())

        @block.sync
        def _(sp):
            lo = Tally()

            def load(src, kt=KT, slot=0, free=True):
                n = lo.up()
                if free:
                    sp.wait_ge(w_lo_done, n - 2)
                sp.dma_start(w_raw[:, slot, 0:kt, :], src).then_inc(raw_landed[slot], 16)

            for c in range(C):
                sp.dma_start(x_tok[:, c, :], x[0, c * P:(c + 1) * P, :]).then_inc(x_landed[c], 16)
            load(w_in[:, :, AT_B:AT_B + P], slot=0, free=False)
            for n, page in enumerate(PAGES):
                for at, src in page:
                    sp.dma_start(pages[at:at + src.shape[0], n, :], src).then_inc(params_landed, 16)
            sp.dma_start(wdt_raw[:], w_in[:, :, AT_DT:AT_DT + HEADS]).then_inc(small_landed, 16)
            sp.dma_start(a_log_b[:], ssd_A_log[0].partition_broadcast(P)).then_inc(small_landed, 16)
            sp.dma_start(dt_bias_b[:], ssd_dt_bias[0].partition_broadcast(P)).then_inc(small_landed, 16)
            sp.dma_start(d_b[:], ssd_D[0].partition_broadcast(P)).then_inc(small_landed, 16)

            def group_loads(g, first):
                if not first:
                    load(w_in[:, :, bass.ds(g * P + (AT_B - P), P)], slot=0)
                load(w_in[:, :, bass.ds(g * P + (AT_C - P), P)], slot=1, free=not first)
                if first:
                    for j in range(XG):
                        load(w_in[:, :, AT_X + j * P:AT_X + (j + 1) * P], slot=j % 2)
                    sp.wait_ge(acs_stored, 16)
                    sp.wait_ge(acs_tok_done, 1)
                sp.wait_ge(exps_done, EXPS * g + (1 - EXPS))
                sp.dma_start(acs_b[:], acs_dram[bass.ds(g * HG - HG, HG), :].partition_broadcast(P)).then_inc(acs_landed, 16)
                for j in range(0 if first else XG):
                    load(w_in[:, :, bass.ds(g * (XG * P) + (AT_X + (j - XG) * P), P)], slot=j % 2)
                for j in range(XG):
                    load(w_in[:, :, bass.ds(g * (XG * P) + (j - XG) * P, P)], slot=j % 2)

            group_loads(1, True)
            with turns(sp, 2, GROUPS + 1, {lo: 6}) as g:
                group_loads(g, False)
            for half in range(2):
                for o in range(2):
                    load(w_out[:, half * KT:(half + 1) * KT, o * P:(o + 1) * P], slot=o)
            with turns(sp, 3, DT + 1, {lo: 2}) as o:
                for half in range(2):
                    load(w_out[:, half * KT:(half + 1) * KT, bass.ds((o - 1) * P, P)], slot=half)
            for layer in range(DEPTH):
                if layer == 1:
                    with turns(sp, 1, WT // 2 + 1, {lo: 6}) as i:
                        for n, part in enumerate((1, 2, 0, 1, 2, 0)):
                            load(w_sc[:, :, bass.ds(i * (2 * P) + ((n // 3 - 2) * P + part * W), P)], slot=n % 2)
                    with turns(sp, 1, DT // 2 + 1, {lo: 2}) as i:
                        for n in range(2):
                            load(w_sc_out[:, :, bass.ds(i * (2 * P) + (n - 2) * P, P)], slot=n)
                with turns(sp, 1, FT + 1, {lo: 2}) as t:
                    for n in range(2):
                        load(w_up[layer][:, :, bass.ds(t * P + (n * HIDDEN - P), P)], slot=n)
                with turns(sp, 1, DT // 2 + 1, {lo: 6}) as i:
                    for n in range(6):
                        part = n % 3
                        load(w_down[layer][:, part * KT:part * KT + DOWN[part], bass.ds(i * (2 * P) + (n // 3 - 2) * P, P)],
                             DOWN[part], slot=n % 2)
            PIECES = [0, 2, 4, 6, 7, 8]
            for at, to in zip(PIECES, PIECES[1:]):
                sp.wait_ge(out_ready, to)
                cols = slice(at * P, to * P)
                sp.dma_start(out[0].rearrange("(c p) n -> p c n", p=P)[:, :, cols], out_tok[:, :, cols]).then_inc(out_stored, 16)
            sp.wait_ge(out_stored, 16 * (len(PIECES) - 1))



        @block.gpsimd
        def _(pool):
            pool.memset(eps[:], EPS).then_inc(consts_done, 1)
            for part in (wdt_hi, wdt_lo):
                pool.memset(part[:].bitcast(F32)[:, :, HEADS:], 0.0).then_inc(wdt_cleared, 1)
            pool.memset(ones[:], 1.0).then_inc(consts_done, 1)
            pool.wait_ge(consts_done, 2)
            pool.affine_select(out=ident[:], in_=ones[:], compare_op=ALU.is_equal, fill=0.0, base=0,
                               pattern=[[-1, P]], channel_multiplier=1).then_inc(consts_done, 1)
            pool.affine_select(out=tri[:], in_=ones[:], compare_op=ALU.is_ge, fill=0.0, base=0,
                               pattern=[[1, P]], channel_multiplier=-1).then_inc(consts_done, 1)
            done, sq = Tally(), Tally()
            norms = 0

            def clear():
                if norms:
                    pool.wait_ge(norm_mm, norms)
                pool.memset(total[:], 0.0).then_inc(summed, 1)
                done.up()

            def add(src):
                pool.wait_ge(squared, sq.up())
                pool.wait_ge(summed, done.now())
                pool.tensor_tensor(total[:].unsqueeze(1), total[:].unsqueeze(1), src, ALU.add).then_inc(summed, 1)
                done.up()

            for tiles in [IT] + [DT] * 4:
                clear()
                with turns(pool, 0, tiles // 2 - 1, {done: 2, sq: 2}):
                    add(square[:, 0:1, :])
                    add(square[:, 1:2, :])
                add(square[:, 0:1, :])
                sq.up()
                norms += 1
                if norms == 1:
                    continue
                if norms < 8:
                    clear()
                pool.wait_ge(m_done, norms // 2 * DT)
                pool.wait_ge(row_done, norms)
                for k in range(HERE if norms < 8 else HERE_LAST, DT):
                    pool.tensor_tensor(m[:, k, :], m[:, k, :], r_post[:], ALU.mult).then_inc(upper_scaled, 1)
                if norms < 8:
                    sq.up(PE_SUMS)
                    with turns(pool, PE_SUMS, DT, {done: 1, sq: 1}) as k:
                        add(squares[:, bass.ds(k, 1), :])
                    norms += 1

        @block.scalar
        def _(act):
            hi, lands, units = Tally(), [Tally(), Tally()], Tally()
            sq, conv, silu, acc_n, gate_n = Tally(), Tally(), Tally(), Tally(), Tally()
            xd, mm_norm, side = Tally(), Tally(), Tally()

            def split_half(n):
                slot = (hi.start + hi.count) % 2
                act.wait_ge(raw_landed[slot], 16 * (lands[slot].now() + 1))
                act.wait_ge(half_unit_done, n)
                nc.scalar.activation(w_hi[:, slot, 0:HALF, :], w_raw[:, slot, 0:HALF, :], ACT.Copy).then_inc(half_hi_done, 1)

            def split(kt=KT, k0=0):
                slot = (hi.start + hi.count) % 2
                n = hi.up()
                act.wait_ge(raw_landed[slot], 16 * lands[slot].up())
                if units.i is not None or units.now() > 0:
                    act.wait_ge(unit_done, units.now())
                nc.scalar.activation(w_hi[:, slot, k0:kt, :], w_raw[:, slot, k0:kt, :], ACT.Copy).then_inc(w_hi_done, 1)

            def unit_ends(kt=KT, k0=0):
                units.up()
                if kt:
                    split(kt, k0)
                else:
                    act.wait_ge(unit_done, units.now())

            SPLITS = {hi: 1, units: 1, lands[0]: 0.5, lands[1]: 0.5}

            def per(n, **more):
                return {t: int(k * n) for t, k in SPLITS.items()}

            def square_of(src, n, ahead=1):
                act.wait_ge(summed, sq.up() - ahead)
                nc.scalar.activation(square[:, n % 2, :], src, ACT.Square).then_inc(squared, 1)

            def root(n):
                act.wait_ge(norm_mm, mm_norm.up())
                nc.scalar.activation(rms_tok[:], bank[6][:, 0:C], ACT.Sqrt, bias=eps[:], scale=1.0 / n).then_inc(root_done, 1)

            def keep_row(dst):
                act.wait_ge(row_mm, mm_norm.now())
                nc.scalar.copy(dst, bank[7][:]).then_inc(row_done, 1)

            def load_roots(n):
                nc.scalar.activation(unread[:, n:n + 1], eps[:], ACT.Sqrt)

            act.wait_ge(consts_done, 1)
            load_roots(0)
            for c in range(C):
                act.wait_ge(x_landed[c], 16)
                nc.scalar.activation(xn_tok[:, c, :], x_tok[:, c, :], ACT.Square, accum_out=sum_sq[:, c:c + 1]).then_inc(x_squared, 1)
                act.wait_ge(x_squared, c + 1)
                nc.scalar.activation(r_tok[:, c:c + 1], sum_sq[:, c:c + 1], ACT.Sqrt, bias=eps[:], scale=1.0 / D).then_inc(r_tok_root, 1)
            split()
            act.wait_ge(pages_turned, 1)
            for n in range(4):
                last = nc.scalar.copy(par[:, n, 0:ROWS[n]], bank[6][:, n * P:n * P + ROWS[n]])
            last.then_inc(par_done, 1)
            act.wait_ge(small_landed, 64)
            act.wait_ge(wdt_cleared, 2)
            nc.scalar.activation(wdt_hi[:, :, 0:HEADS], wdt_raw[:], ACT.Copy).then_inc(wdt_split, 1)
            act.wait_ge(par_done, 1)
            for k in range(DT):
                act.wait_ge(xn_done, k + 1)
                nc.scalar.activation(h_hi[:, k, :], bank[2 + k % 4][:], ACT.Copy, scale=one(col_gain(MIX_PRE, 0, k))).then_inc(h_hi_done, 1)
            split()
            act.wait_ge(dt_row_mm, 1)
            nc.scalar.copy(dt_row[:], bank[7][0:HEADS, :]).then_inc(dt_row_done, 1)
            act.wait_ge(dt_vec, 1)
            nc.scalar.activation(dt_e[:], dt_u[:], ACT.Abs).then_inc(dt_act, 1)
            act.wait_ge(dt_act, 1)
            nc.scalar.activation(dt_e[:], dt_e[:], ACT.Exp, scale=-1.0).then_inc(dt_act, 1)
            nc.scalar.activation(a_log_b[:], a_log_b[:], ACT.Exp).then_inc(dt_act, 1)
            act.wait_ge(dt_act, 3)
            nc.scalar.activation(dt_e[:], dt_e[:], ACT.Ln, bias=1.0).then_inc(dt_act, 1)
            act.wait_ge(acs_mm, 1)
            nc.scalar.copy(acs_row[:], bank[2][0:HEADS, :]).then_inc(acs_row_done, 1)
            act.wait_ge(acs_row_done, 1)
            act.dma_start(acs_dram, acs_row[:]).then_inc(acs_stored, 16)
            nc.scalar.copy(decay[:, 0, 0:1], eps[:]).then_inc(exps_done, 1)
            unit_ends()
            for k in range(0, DT, 2):
                act.wait_ge(x_turned, k + 1)
                nc.scalar.copy(xs[:, k, :], bank[4][:]).then_inc(xs_done[0], 1)
            act.wait_ge(pads_done, 1)

            def conv_in(page_tile, f):
                if f:
                    unit_ends()
                if f >= 2:
                    act.wait_ge(conv_step, conv.now() + (f - 1) * (SSD_CW - 1))
                u = mm_of(f)
                nc.scalar.copy(pad[:, f % 2, SSD_CW - 1:], u)
                nc.scalar.activation(feat[:, f, :], u, ACT.Identity, bias=one(col_ssd_b(page_tile)),
                                     scale=one(col_ssd_w(SSD_CW - 1, page_tile))).then_inc(evicted, 1)

            def conv_out(f):
                act.wait_ge(conv_step, conv.now() + (f + 1) * (SSD_CW - 1))
                nc.scalar.activation(feat[:, f, :], feat[:, f, :], ACT.Silu).then_inc(silu_done, 1)

            def mm_of(n):
                return bank[GROUP_BANKS[n]][:]

            seg, bt, st, ymm, yst = Tally(), Tally(), Tally(), Tally(), Tally()
            exps = Tally()
            exps.up()
            with turns(act, 0, GROUPS, per(6) | {conv: 12, seg: 1, bt: 2, st: 2, yst: 8, sq: 2, exps: EXPS}) as g:
                conv_in(CONV_T - 2 * GROUPS + g, 0)
                conv_in(CONV_T - GROUPS + g, 1)
                act.wait_ge(seg_done, seg.up())
                nc.scalar.activation(mask[:], mask[:], ACT.Exp).then_inc(exps_done, 1)
                for j in range(XG):
                    for h in range(HX):
                        rows = slice(h * HD, (h + 1) * HD)
                        nc.scalar.activation(e_row[rows, j, :], acs_b[rows, j * HX + h, P:], ACT.Exp).then_inc(exps_done, 1)
                nc.scalar.activation(decay[:], decay[:], ACT.Exp).then_inc(exps_done, 1)
                nc.scalar.activation(c_decay[:], acs_b[:].rearrange("p h (c l) -> p h c l", l=P)[:, :, 0:C - 1, P - 1],
                                     ACT.Exp).then_inc(exps_done, 1)
                exps.up(EXPS)
                conv_in(g * XG, 2)
                conv_out(0)
                conv_out(1)
                conv_in(g * XG + 1, 3)
                conv_out(2)
                act.wait_ge(cb_turned, bt.up(2))
                nc.scalar.copy(b_tok[:], bank[3][:, 0:LATER]).then_inc(b_tok_done, 1)
                conv_out(3)
                conv.up(4 * (SSD_CW - 1))
                unit_ends()
                nc.scalar.activation(z_act[:, 0, :], bank[0][:], ACT.Silu).then_inc(evicted, 1)
                act.wait_ge(unit_done, units.now() + 1)
                nc.scalar.activation(z_act[:, 1, :], bank[1][:], ACT.Silu).then_inc(evicted, 1)
                act.wait_ge(states_mm, st.up())
                nc.scalar.copy(prev[:, 0, :], bank[6][:, 0:HG * HD]).then_inc(prev0_done, 1)
                st.up()
                unit_ends()
                for j in range(XG):
                    act.wait_ge(y_step, yst.up(4))
                    nc.scalar.activation(y_hi[:, bass.ds(g * XG + j, 1), :], feat[:, 2 + j, :], ACT.Copy,
                                         scale=one(col_norm_w(g * XG + j))).then_inc(y_hi_done, 1)
                    square_of(feat[:, 2 + j, :], j, ahead=0)
                unit_ends()

            md = Tally()

            def out_proj(o, first):
                for j in range(2):
                    if not (first and j == 0):
                        unit_ends()
                    unit_ends()
                    if first and j == 0:
                        root(INNER)
                        keep_row(r_post[:])
                    act.wait_ge(m_done, md.up())
                    square_of(m[:, bass.ds(2 * o + j, 1), :], j)

            out_proj(0, True)
            with turns(act, 1, DT // 2, per(4) | {md: 2, sq: 2}) as o:
                out_proj(o, False)

            def boundary(nth, pre):
                root(D)
                act.wait_ge(scaled_done, (nth - 1) * HERE + 1)
                keep_row(r_post[:])
                if not pre:
                    return
                with turns(act, 0, DT // 2, {xd: 2}) as i:
                    for n in range(2):
                        k = 2 * i + n
                        act.wait_ge(x_done, xd.up())
                        nc.scalar.activation(h_hi[:, bass.ds(k, 1), :], xs[:, bass.ds(k, 1), :], ACT.Copy,
                                             scale=one(col_gain(*pre, k))).then_inc(h_hi_done, 1)
                        nc.scalar.activation(squares[:, bass.ds(k, 1), :], xs[:, bass.ds(k, 1), :], ACT.Square).then_inc(squared, 1)
                sq.up(DT - PE_SUMS + 1)
                split_half(nth)

            def ffn_up(layer, t, first):
                if first:
                    unit_ends(k0=HALF)
                    unit_ends()
                    root(D)
                    keep_row(r_pre[:])
                for j in range(2):
                    if not (first and j == 0):
                        unit_ends()
                    act.wait_ge(gate_in, gate_n.up())
                    nc.scalar.activation(acc[:], cpad[:, CW - 1:], ACT.Identity, bias=one(col_ffn_b(layer, 2 * t + j)),
                                         scale=one(col_ffn_w(layer, CW - 1, 2 * t + j))).then_inc(acc_done, 1)
                    if first and j == 0:
                        unit_ends()
                    act.wait_ge(conv_step, conv.up(CW - 1))
                    nc.scalar.activation(acc[:], acc[:], ACT.Silu).then_inc(silu_done, 1)
                    if not first:
                        unit_ends()
                    act.wait_ge(side_step, side.up(2))
                    nc.scalar.activation(hid_hi[:, bass.ds(2 * t + j, 1), :], gated[:], ACT.Copy).then_inc(hid_hi_done, 1)

            def ffn_down(o, last):
                for j in range(2):
                    unit_ends(DOWN[2])
                    unit_ends(0 if last and j else DOWN[0])
                    act.wait_ge(unit_done, units.now() + 1)
                    square_of(bank[4 + j][:], j)
                    nc.scalar.copy(m[:, bass.ds(2 * o + j, 1), :], bank[4 + j][:]).then_inc(m_done, 1)
                    md.up()
                    unit_ends(0 if last and j else DOWN[1])

            for layer in range(DEPTH):
                if layer == 1:
                    boundary(2, (MIX_PRE, 1))

                    def sc_in(i, first):
                        for j in range(2):
                            unit_ends(k0=HALF if first and j == 0 else 0)
                            unit_ends()
                            if first and j == 0:
                                root(D)
                                keep_row(r_pre[:])
                            act.wait_ge(gate_in, gate_n.up())
                            nc.scalar.activation(acc[:], cpad[:, CW - 1:], ACT.Copy,
                                                 scale=one(col_sc_w(CW - 1, 2 * i + j))).then_inc(acc_done, 1)
                            unit_ends()
                            conv.up(CW - 1)
                            act.wait_ge(side_step, side.up(3))
                            nc.scalar.activation(hid_hi[:, bass.ds(2 * i + j, 1), :], gated[:], ACT.Copy).then_inc(hid_hi_done, 1)

                    sc_in(0, True)
                    with turns(act, 1, WT // 2, per(6) | {gate_n: 2, conv: 4, side: 6}) as i:
                        sc_in(i, False)
                    with turns(act, 0, DT // 4, per(4) | {md: 4, sq: 4}) as i:
                        for j in range(4):
                            act.wait_ge(unit_done, units.now() + 1)
                            square_of(bank[j][:], j)
                            nc.scalar.copy(m[:, bass.ds(4 * i + j, 1), :], bank[j][:]).then_inc(m_done, 1)
                            md.up()
                            unit_ends()
                boundary(2 * layer + 1, (FFN_PRE, layer))
                ffn_up(layer, 0, True)
                with turns(act, 1, FT // 2, per(4) | {gate_n: 2, conv: 4, side: 4}) as t:
                    ffn_up(layer, t, False)
                load_roots(1 + layer)
                last_turn = 1 if layer == DEPTH - 1 else 0
                with turns(act, 0, DT // 2 - last_turn, per(6) | {md: 2, sq: 2}) as o:
                    ffn_down(o, False)
                if last_turn:
                    ffn_down(DT // 2 - 1, True)
            boundary(4, None)
            for k in range(DT):
                act.wait_ge(out_turned, k + 1)
                nc.scalar.copy(out_tok[:, :, k * P:(k + 1) * P], bank[k % 4][:].rearrange("p (c l) -> p c l", l=P)).then_inc(out_ready, 1)

        @block.vector
        def _(dve):
            lo, units = Tally(), Tally()
            ev, cs, hh, xdn, roots, rows = (Tally() for _ in range(6))
            scaled, upper, mdn = Tally(), Tally(), Tally()
            taken = Tally()

            def lower(slot, k0, kt):
                return nc.vector.tensor_tensor(w_lo[:, slot, k0:kt, :], w_raw[:, slot, k0:kt, :],
                                               w_hi[:, slot, k0:kt, :].bitcast(F32), ALU.subtract)

            def split_half(n):
                dve.wait_ge(half_hi_done, n)
                lower((lo.start + lo.count) % 2, 0, HALF).then_inc(half_lo_done, 1)

            def split(kt=KT, k0=0):
                slot = (lo.start + lo.count) % 2
                dve.wait_ge(w_hi_done, lo.up())
                lower(slot, k0, kt).then_inc(w_lo_done, 1)

            def unit_ends(kt=KT, k0=0):
                units.up()
                if kt:
                    split(kt, k0)

            def rstd(kept, kt=0):
                dve.wait_ge(root_done, roots.up())
                nc.vector.reciprocal(rms_tok[:], rms_tok[:]).then_inc(rstd_done, 1)
                if kt:
                    unit_ends(kt)
                if kept:
                    dve.wait_ge(row_done, rows.up())
                else:
                    dve.wait_ge(row_mm, roots.now())

            for c in range(C):
                dve.wait_ge(r_tok_root, c + 1)
                nc.vector.reciprocal(r_tok[:, c:c + 1], r_tok[:, c:c + 1]).then_inc(r_tok_done, 1)
                dve.wait_ge(r_tok_done, c + 1)
                nc.vector.tensor_scalar(xn_tok[:, c, :], x_tok[:, c, :], r_tok[:, c:c + 1], None, ALU.mult).then_inc(xn_ready, 1)
            split()
            dve.wait_ge(wdt_split, 1)
            nc.vector.tensor_tensor(wdt_lo[:, :, 0:HEADS], wdt_raw[:], wdt_hi[:, :, 0:HEADS].bitcast(F32), ALU.subtract).then_inc(wdt_split, 1)
            dve.wait_ge(par_done, 1)
            for k in range(DT):
                dve.wait_ge(h_hi_done, hh.up())
                nc.vector.scalar_tensor_tensor(out=h_lo[:, k, :], in0=bank[2 + k % 4][:], scalar=one(col_gain(MIX_PRE, 0, k)),
                                               in1=h_hi[:, k, :].bitcast(F32), op0=ALU.mult, op1=ALU.subtract).then_inc(h_lo_done, 1)
            split()
            flat = "p (c h) -> p c h"
            dve.wait_ge(dt_mm, 1)
            nc.vector.tensor_tensor(dt_u[:].rearrange(flat, c=C), bank[4][:, 0:C * HEADS].rearrange(flat, c=C),
                                    dt_bias_b[:].unsqueeze(1).to_broadcast([P, C, HEADS]), ALU.add).then_inc(dt_vec, 1)
            dve.wait_ge(dt_act, 4)
            nc.vector.scalar_tensor_tensor(out=dt_tok[:].rearrange("p c h -> p (c h)"), in0=dt_u[:], scalar=0.0, in1=dt_e[:],
                                           op0=ALU.max, op1=ALU.add).then_inc(dt_vec, 1)
            dve.wait_ge(dt_vec, 2)
            nc.vector.scalar_tensor_tensor(out=a_tok[:].rearrange(flat, c=C), in0=dt_tok[:], scalar=-1.0,
                                           in1=a_log_b[:].unsqueeze(1).to_broadcast([P, C, HEADS]),
                                           op0=ALU.mult, op1=ALU.mult).then_inc(dt_vec, 1)
            nc.vector.memset(pad[:, :, 0:SSD_CW - 1], 0.0).then_inc(pads_done, 1)
            dve.wait_ge(small_landed, 64)
            for h in range(HX):
                nc.vector.tensor_copy(d_col[h * HD:(h + 1) * HD, :], d_b[h * HD:(h + 1) * HD, :].rearrange("p (t h) -> p h t", h=HX)[:, h, :])
            dve.wait_ge(acs_mm, 2)
            nc.vector.tensor_copy(acs_tok[:].rearrange("p c h -> p (c h)"), bank[3][:, 0:C * HEADS]).then_inc(acs_tok_done, 1)
            dve.wait_ge(acs_tok_done, 1)
            unit_ends()
            for k in range(1, DT, 2):
                dve.wait_ge(x_turned, k + 1)
                nc.vector.tensor_copy(xs[:, k, :], bank[5][:]).then_inc(xs_done[1], 1)
            al, sd, ex, cb, ms, xt, st, p0, ss, ym, ys, yh = (Tally() for _ in range(12))
            ex.up()
            sd.up()

            def conv(f, page_tile):
                if f >= 2:
                    unit_ends()
                dve.wait_ge(evicted, ev.up())
                for tap in range(SSD_CW - 1):
                    if tap:
                        dve.wait_ge(conv_step, cs.now())
                    nc.vector.scalar_tensor_tensor(out=feat[:, f, :], in0=pad[:, f % 2, tap:tap + T],
                                                   scalar=one(col_ssd_w(tap, page_tile)), in1=feat[:, f, :],
                                                   op0=ALU.mult, op1=ALU.add).then_inc(conv_step, 1)
                    cs.up()

            def by_head(ap):
                return ap.rearrange("p (h e) -> p h e", e=HD)

            with turns(dve, 0, GROUPS, {lo: 6, units: 6, ev: 6, cs: 12, al: 1, sd: 1, ex: EXPS, cb: 1, ms: 2, xt: 2,
                                        st: 2, p0: 1, ss: 4, ym: 2, ys: 8, yh: 2}) as g:
                dve.wait_ge(acs_landed, 16 * al.up())
                nc.vector.tensor_tensor(decay[:], acs_b[:].rearrange("p h (c l) -> p h c l", l=P)[:, :, 0:C - 1, P - 1],
                                        acs_tok[:, 0:C - 1, bass.ds(g * HG, HG)].rearrange("p c h -> p h c"), ALU.subtract)
                dve.wait_ge(scan_done, sd.now())
                sd.up()
                for h in range(HG):
                    for c in range(C):
                        span = slice(c * P, (c + 1) * P)
                        last = nc.vector.tensor_scalar(mask[:, h, span], acs_b[:, h, span], acs_tok[:, c, bass.ds(g * HG + h, 1)],
                                                       0.0, ALU.subtract, ALU.min)
                last.then_inc(seg_done, 1)
                unit_ends()
                conv(0, CONV_T - 2 * GROUPS + g)
                conv(1, CONV_T - GROUPS + g)
                conv(2, g * XG)
                conv(3, g * XG + 1)
                dve.wait_ge(cb_turned, cb.now() * 2 + 1)
                cb.up()
                nc.vector.tensor_tensor(cbm[:].rearrange("p (c l) -> p c l", l=P), bank[2][:].rearrange("p (c l) -> p c l", l=P),
                                        tri[:].unsqueeze(1).to_broadcast([P, C, P]), ALU.mult).then_inc(mask_step, 1)
                dve.wait_ge(mask_step, ms.up())
                dve.wait_ge(exps_done, ex.up(EXPS))
                nc.vector.tensor_tensor(mask[:], mask[:], cbm[:].unsqueeze(1).to_broadcast([P, HG, T]), ALU.mult).then_inc(mask_step, 1)
                ms.up()
                unit_ends()
                for j in range(XG):
                    dve.wait_ge(x_tok_turned, xt.up())
                    nc.vector.tensor_tensor(
                        xdt[:, :, j * P:(j + 1) * P].rearrange("p c (h e) -> p c h e", e=HD),
                        bank[4 + j][:].rearrange("p (c h e) -> p c h e", c=C, e=HD),
                        dt_tok[:, :, bass.ds(g * HG + j * HX, HX)].unsqueeze(3).to_broadcast([P, C, HX, HD]),
                        ALU.mult).then_inc(xdt_done, 1)
                dve.wait_ge(xdt_done, (xt.now() // 2) * 3 - 1 if xt.i is None else xt.i * 3 + 2)
                nc.vector.tensor_tensor(
                    xdd[:].rearrange("p c (h e) -> p c h e", e=HD),
                    xdt[:, 0:C - 1, :].rearrange("p c (h e) -> p c h e", e=HD),
                    decay[:].rearrange("p h c -> p c h").unsqueeze(3).to_broadcast([P, C - 1, HG, HD]),
                    ALU.mult).then_inc(xdt_done, 1)
                dve.wait_ge(states_mm, st.up(2))
                dve.wait_ge(prev0_done, p0.up())
                for c in range(1, C - 1):
                    if c > 1:
                        dve.wait_ge(state_step, ss.now())
                    nc.vector.tensor_tensor(by_head(prev[:, c, :]), by_head(prev[:, c - 1, :]),
                                            c_decay[:, :, c:c + 1].to_broadcast([P, HG, HD]), ALU.mult).then_inc(state_step, 1)
                    dve.wait_ge(state_step, ss.up())
                    nc.vector.tensor_tensor(prev[:, c, :], prev[:, c, :],
                                            bank[6 + c // 2][:, c % 2 * HG * HD:(c % 2 + 1) * HG * HD], ALU.add).then_inc(state_step, 1)
                    ss.up()
                unit_ends()
                dve.wait_ge(evicted, ev.up(2))
                for j in range(XG):
                    dve.wait_ge(y_mm, ym.up())
                    nc.vector.tensor_tensor(e_row[:, j, :], e_row[:, j, :], bank[2 + j][:, P:], ALU.mult).then_inc(y_step, 1)
                    nc.vector.scalar_tensor_tensor(out=feat[:, 2 + j, :], in0=feat[:, 2 + j, :],
                                                   scalar=d_col[:, bass.ds(g * XG + j, 1)], in1=bank[4 + j][:],
                                                   op0=ALU.mult, op1=ALU.add).then_inc(y_step, 1)
                    dve.wait_ge(y_step, ys.up(2))
                    nc.vector.tensor_tensor(feat[:, 2 + j, P:], feat[:, 2 + j, P:], e_row[:, j, :], ALU.add).then_inc(y_step, 1)
                    dve.wait_ge(y_step, ys.up())
                    nc.vector.tensor_tensor(feat[:, 2 + j, :], feat[:, 2 + j, :], z_act[:, j, :], ALU.mult).then_inc(y_step, 1)
                    ys.up()
                for j in range(XG):
                    dve.wait_ge(y_hi_done, yh.up())
                    nc.vector.scalar_tensor_tensor(out=y_lo[:, bass.ds(g * XG + j, 1), :], in0=feat[:, 2 + j:3 + j, :],
                                                   scalar=one(col_norm_w(g * XG + j)), in1=y_hi[:, bass.ds(g * XG + j, 1), :].bitcast(F32),
                                                   op0=ALU.mult, op1=ALU.subtract).then_inc(y_lo_done, 1)
                unit_ends()

            def out_proj(o, first, last):
                for j in range(2):
                    unit_ends()
                    if first and j == 0:
                        rstd(True)
                    dve.wait_ge(unit_done, units.now() + 1)
                    nc.vector.tensor_tensor(m[:, bass.ds(2 * o + j, 1), :], bank[j][:].unsqueeze(1), r_post[:].unsqueeze(1),
                                            ALU.mult).then_inc(m_done, 1)
                    mdn.up()
                    if not (first and j == 0 or last and j == 1):
                        unit_ends()

            out_proj(0, True, False)
            with turns(dve, 1, DT // 2 - 1, {lo: 4, units: 4, mdn: 2}) as o:
                out_proj(o, False, False)
            out_proj(DT // 2 - 1, False, True)

            def scale(k, row):
                nc.vector.tensor_tensor(side[:, k % 2, :], m[:, k, :], row, ALU.mult).then_inc(scaled_done, 1)

            def residual(k, here, layer, which):
                if k < here:
                    dve.wait_ge(scaled_done, scaled.up())
                else:
                    dve.wait_ge(upper_scaled, upper.up())
                nc.vector.scalar_tensor_tensor(out=xs[:, k, :], in0=side[:, k % 2, :] if k < here else m[:, k, :],
                                               scalar=one(col_gain(which, layer, k)), in1=xs[:, k, :],
                                               op0=ALU.mult, op1=ALU.add).then_inc(x_done, 1)
                xdn.up()

            def low(k, layer, which):
                dve.wait_ge(h_hi_done, hh.up())
                nc.vector.scalar_tensor_tensor(out=h_lo[:, k, :], in0=xs[:, k, :], scalar=one(col_gain(which, layer, k)),
                                               in1=h_hi[:, k, :].bitcast(F32), op0=ALU.mult, op1=ALU.subtract).then_inc(h_lo_done, 1)

            def boundary(nth, post, pre):
                rstd(False, KT if pre else 0)
                dve.wait_ge(m_done, mdn.now())
                scale(0, bank[7][:])
                here = HERE if pre else HERE_LAST
                residual(0, here, *post)
                dve.wait_ge(row_done, rows.up())
                scale(1, r_post[:])
                for k in range(1, DT):
                    def scale_next():
                        if k + 1 < here:
                            dve.wait_ge(x_done, xdn.now())
                            scale(k + 1, r_post[:])

                    if k > 1:
                        scale_next()
                    residual(k, here, *post)
                    if pre:
                        low(k - 1, *pre)
                    if k == 1:
                        scale_next()
                if pre:
                    low(DT - 1, *pre)
                    split_half(nth)

            hd, ac, sl, st2 = Tally(), Tally(), Tally(), Tally()
            sl.up(4 * GROUPS)

            def conv_taps(cols):
                dve.wait_ge(acc_done, ac.up())
                for tap in range(CW - 1):
                    if tap:
                        dve.wait_ge(conv_step, cs.now())
                    nc.vector.scalar_tensor_tensor(out=acc[:], in0=cpad[:, tap:tap + T], scalar=one(cols(tap)), in1=acc[:],
                                                   op0=ALU.mult, op1=ALU.add).then_inc(conv_step, 1)
                    cs.up()

            def low_hidden(t):
                dve.wait_ge(hid_hi_done, hd.up())
                nc.vector.tensor_tensor(hid_lo[:, bass.ds(t, 1), :], gated[:].unsqueeze(1), hid_hi[:, bass.ds(t, 1), :].bitcast(F32),
                                        ALU.subtract).then_inc(hid_lo_done, 1)

            def ffn_up(layer, t, first):
                if first:
                    unit_ends(k0=HALF)
                    unit_ends()
                    rstd(True)
                for j in range(2):
                    dve.wait_ge(unit_done, taken.up())
                    nc.vector.tensor_tensor(cpad[:, CW - 1:], bank[2 * j][:], r_pre[:], ALU.mult).then_inc(gate_in, 1)
                    unit_ends()
                    conv_taps(lambda tap: col_ffn_w(layer, tap, 2 * t + j))
                    dve.wait_ge(unit_done, taken.up())
                    nc.vector.tensor_tensor(side[:, 0, :], bank[2 * j + 1][:], r_pre[:], ALU.mult).then_inc(side_step, 1)
                    if not first:
                        unit_ends()
                    dve.wait_ge(side_step, st2.up())
                    dve.wait_ge(silu_done, sl.up())
                    nc.vector.tensor_tensor(gated[:], side[:, 0, :], acc[:], ALU.mult).then_inc(side_step, 1)
                    st2.up()
                    low_hidden(2 * t + j)

            def sc_in(i, first):
                if first:
                    unit_ends(k0=HALF)
                    unit_ends()
                    rstd(True)
                    nc.vector.tensor_tensor(r_pre2[:], r_pre[:], r_pre[:], ALU.mult).then_inc(pre2_done, 1)
                    dve.wait_ge(pre2_done, 1)
                for j in range(2):
                    dve.wait_ge(unit_done, taken.up())
                    nc.vector.tensor_tensor(side[:, 0, :], bank[3 * j][:], r_pre2[:], ALU.mult).then_inc(side_step, 1)
                    if not (first and j == 0):
                        unit_ends()
                    dve.wait_ge(side_step, st2.up())
                    dve.wait_ge(unit_done, taken.up())
                    nc.vector.tensor_tensor(cpad[:, CW - 1:], side[:, 0, :], bank[3 * j + 1][:], ALU.mult).then_inc(gate_in, 1)
                    if not (first and j == 0):
                        unit_ends()
                    conv_taps(lambda tap: col_sc_w(tap, 2 * i + j))
                    dve.wait_ge(unit_done, taken.up())
                    nc.vector.tensor_tensor(side[:, 0, :], bank[3 * j + 2][:], r_pre[:], ALU.mult).then_inc(side_step, 1)
                    unit_ends()
                    dve.wait_ge(side_step, st2.up())
                    dve.wait_ge(conv_step, cs.now())
                    nc.vector.tensor_tensor(gated[:], side[:, 0, :], acc[:], ALU.mult).then_inc(side_step, 1)
                    st2.up()
                    low_hidden(2 * i + j)

            for layer in range(DEPTH):
                if layer == 1:
                    boundary(2, (0, FFN_POST), (1, MIX_PRE))
                    taken.count += units.now() - taken.now()
                    sc_in(0, True)
                    with turns(dve, 1, WT // 2, {lo: 6, units: 6, taken: 6, cs: 4, ac: 2, hd: 2, st2: 6}) as i:
                        sc_in(i, False)
                    for n in range(DT - 1):
                        unit_ends()
                    mdn.up(DT)
                else:
                    nc.vector.memset(cpad[:, 0:CW - 1], 0.0).then_inc(pads_done, 1)
                    dve.wait_ge(pads_done, 2)
                boundary(2 * layer + 1, (layer, MIX_POST), (layer, FFN_PRE))
                taken.count += units.now() - taken.now()
                ffn_up(layer, 0, True)
                with turns(dve, 1, FT // 2, {lo: 4, units: 4, taken: 4, cs: 4, ac: 2, hd: 2, st2: 4, sl: 2}) as t:
                    ffn_up(layer, t, False)
                with turns(dve, 0, DT // 2 - 1, {lo: 6, units: 6}):
                    for n in range(6):
                        unit_ends(DOWN[(n + 2) % 3])
                for n in range(5 if layer < DEPTH - 1 else 6):
                    unit_ends(DOWN[(n + 2) % 3] if n < 4 else KT if layer < DEPTH - 1 else 0)
                mdn.up(DT)
            boundary(4, (1, FFN_POST), None)

        @block.tensor
        def _(pe):
            lo, sm, sqs, hh, hl, rs = (Tally() for _ in range(6))
            hh.up(DT)

            def three(dst, wh, wl, xh, xl, start, stop):
                nc.tensor.matmul(dst, wh, xh, start=start, stop=False)
                nc.tensor.matmul(dst, wl, xh, start=False, stop=False)
                return nc.tensor.matmul(dst, wh, xl, start=False, stop=stop)

            def unit(dst, in_hi, in_lo, kt=KT, k0=0, start=True, stop=True, by_tile=None, behind={}, halves=0):
                slot = (lo.start + lo.count) % 2
                lo.up()
                if halves:
                    pe.wait_ge(half_lo_done, halves)
                else:
                    pe.wait_ge(w_lo_done, lo.now())
                for k in range(kt):
                    if halves and k == HALF:
                        pe.wait_ge(w_lo_done, lo.now())
                    if by_tile:
                        pe.wait_ge(by_tile[0], by_tile[1] + k + 1)
                    last = three(dst, w_hi[:, slot, k, :], w_lo[:, slot, k, :], in_hi[:, k0 + k, :], in_lo[:, k0 + k, :],
                                 start and k == 0, stop and k == kt - 1)
                    if k in behind:
                        behind[k]()
                last.then_inc(unit_done, 1)

            def two_units(dst0, dst1):
                pe.wait_ge(w_lo_done, lo.up(2))
                for at in range(KT + LAG):
                    for slot, dst, k in ((0, dst0, at), (1, dst1, at - LAG)):
                        if not 0 <= k < KT:
                            continue
                        if slot == 0:
                            pe.wait_ge(h_hi_done, hh.up())
                        nc.tensor.matmul(dst, w_hi[:, slot, k, :], h_hi[:, k, :], start=k == 0, stop=False)
                        nc.tensor.matmul(dst, w_lo[:, slot, k, :], h_hi[:, k, :], start=False, stop=False)
                        if slot == 0:
                            pe.wait_ge(h_lo_done, hl.up())
                        last = nc.tensor.matmul(dst, w_hi[:, slot, k, :], h_lo[:, k, :], start=False, stop=k == KT - 1)
                        if k == KT - 1:
                            last.then_inc(unit_done, 1)
                        if slot == 0 and k == HALF - 1:
                            last.then_inc(half_unit_done, 1)
                    if at < PE_SUMS:
                        add_square(at)

            def norm_sum(tiles, spare=3):
                pe.wait_ge(summed, sm.up(tiles))
                for c in range(C):
                    nc.tensor.matmul(bank[6][:, c:c + 1], total[:, c * P:(c + 1) * P], ones[:, 0:1], start=c == 0, stop=False)
                if tiles == DT:
                    keep_warm(WARM[0], spare)
                pe.wait_ge(squared, sqs.up(tiles))
                for c in range(C):
                    last = nc.tensor.matmul(bank[6][:, c:c + 1], square[:, 1, c * P:(c + 1) * P], ones[:, 0:1], start=False,
                                            stop=c == C - 1)
                last.then_inc(norm_mm, 1)

            def add_square(k):
                pe.wait_ge(squared, sqs.up())
                for c in range(C):
                    nc.tensor.matmul(bank[6][:, c:c + 1], squares[:, k, c * P:(c + 1) * P], ones[:, 0:1], start=k == 0 and c == 0,
                                     stop=False)

            def norm_sum_pre():
                sqs.up(DT - PE_SUMS)
                pe.wait_ge(summed, sm.up(DT - PE_SUMS + 1))
                for c in range(C):
                    last = nc.tensor.matmul(bank[6][:, c:c + 1], total[:, c * P:(c + 1) * P], ones[:, 0:1], start=False,
                                            stop=c == C - 1)
                last.then_inc(norm_mm, 1)

            def norm_row():
                pe.wait_ge(rstd_done, rs.up())
                for c in range(C):
                    last = nc.tensor.transpose(bank[7][:, c * P:(c + 1) * P], rms_tok[:, c:c + 1].to_broadcast([P, P]), ident[:])
                last.then_inc(row_mm, 1)

            def keep_warm(n, spare=3):
                for _ in range(n):
                    nc.tensor.matmul(bank[spare][:, 0:P], tri[:], ones[:], start=True, stop=True)

            def turn_xn(k, c):
                return nc.tensor.transpose(bank[2 + k % 4][:, c * P:(c + 1) * P], xn_tok[:, c, k * P:(k + 1) * P], ident[:])

            pe.wait_ge(consts_done, 4)
            keep_warm(8, 7)
            for c in range(C):
                if c == C - 1:
                    pe.wait_ge(params_landed, 16 * N_PARAM)
                    for n in range(4):
                        last = nc.tensor.transpose(bank[6][:, n * P:n * P + ROWS[n]], pages[0:ROWS[n], n, :], ident[0:ROWS[n], 0:ROWS[n]])
                    last.then_inc(pages_turned, 1)
                else:
                    keep_warm(2, 7)
                pe.wait_ge(xn_ready, c + 1)
                for k in range(4):
                    last = turn_xn(k, c)
                    if c == C - 1:
                        last.then_inc(xn_done, 1)
            keep_warm(6, 7)

            def dt_product(k):
                pe.wait_ge(h_lo_done, hl.up())
                return three(bank[7][:], wdt_hi[:, k, :], wdt_lo[:, k, :], h_hi[:, k, :], h_lo[:, k, :], k == 0, k == DT - 1)

            pe.wait_ge(wdt_split, 2)
            for k in range(4, DT):
                dt_product(k - 4)
                for c in range(C):
                    last = turn_xn(k, c)
                last.then_inc(xn_done, 1)
            ev, si, bt, mk, xd, ss = (Tally() for _ in range(6))

            def group_unit(n, behind={}):
                ev.up()
                if n >= 4:
                    pe.wait_ge(evicted, ev.now() - 2)
                unit(bank[GROUP_BANKS[n]][:], h_hi, h_lo, behind=behind)

            for k in range(DT - 4, DT):
                last = dt_product(k)
            pe.wait_ge(par_done, 1)
            last.then_inc(dt_row_mm, 1)

            def turn_dt():
                pe.wait_ge(dt_row_done, 1)
                for c in range(C):
                    last = nc.tensor.transpose(bank[4][:, c * HEADS:(c + 1) * HEADS], dt_row[:, c * P:(c + 1) * P], ident[0:HEADS, 0:HEADS])
                last.then_inc(dt_mm, 1)

            group_unit(0, behind={1: turn_dt})
            pe.wait_ge(dt_vec, 3)
            for c in range(C):
                last = nc.tensor.matmul(bank[2][0:HEADS, c * P:(c + 1) * P], a_tok[:, c * HEADS:(c + 1) * HEADS], tri[:],
                                        start=True, stop=True)
            last.then_inc(acs_mm, 1)
            nc.tensor.matmul(bank[3][:, 0:C * HEADS], tri[:], a_tok[:], start=True, stop=True).then_inc(acs_mm, 1)

            def turn_x(k):
                if k >= 2:
                    pe.wait_ge(xs_done[k % 2], k // 2)
                for c in range(C):
                    last = nc.tensor.transpose(bank[4 + k % 2][:, c * P:(c + 1) * P], x_tok[:, c, k * P:(k + 1) * P], ident[:])
                last.then_inc(x_turned, 1)

            group_unit(1, behind={k: partial(turn_x, k) for k in range(DT)})
            pe.wait_ge(acs_row_done, 1)
            nc.tensor.transpose(bank[2][:, 0:P], ident[:], ident[:]).then_inc(scan_done, 1)

            def group(last_group):
                group_unit(2)
                group_unit(3)
                pe.wait_ge(silu_done, si.up(2))
                for c in range(C):
                    span = slice(c * P, (c + 1) * P)
                    last = nc.tensor.matmul(bank[2][:, span], feat[:, 0, span], feat[:, 1, span], start=True, stop=True)
                last.then_inc(cb_turned, 1)
                for c in range(C - 1):
                    last = nc.tensor.transpose(bank[3][:, c * P:(c + 1) * P], feat[:, 0, c * P:(c + 1) * P], ident[:])
                last.then_inc(cb_turned, 1)
                group_unit(4)
                for j in range(XG):
                    pe.wait_ge(silu_done, si.up())
                    for c in range(C):
                        last = nc.tensor.transpose(bank[4 + j][:, c * P:(c + 1) * P], feat[:, 2 + j, c * P:(c + 1) * P], ident[:])
                    last.then_inc(x_tok_turned, 1)
                group_unit(5)
                pe.wait_ge(b_tok_done, bt.up())
                pe.wait_ge(xdt_done, xd.up(3))
                for c in range(C - 1):
                    last = nc.tensor.matmul(bank[6 + c // 2][:, c % 2 * HG * HD:(c % 2 + 1) * HG * HD], b_tok[:, c * P:(c + 1) * P],
                                            xdd[:, c, :], start=True, stop=True)
                    if c:
                        last.then_inc(states_mm, 1)
                pe.wait_ge(mask_step, mk.up(2))
                for j in range(XG):
                    for h in range(HX):
                        for c in range(C):
                            cols = slice(j * P + h * HD, j * P + (h + 1) * HD)
                            last = nc.tensor.matmul(bank[4 + j][h * HD:(h + 1) * HD, c * P:(c + 1) * P], xdt[:, c, cols],
                                                    mask[:, j * HX + h, c * P:(c + 1) * P], start=True, stop=True)
                last.then_inc(scan_done, 1)
                pe.wait_ge(prev0_done, bt.now())
                pe.wait_ge(state_step, ss.up(4))
                for j in range(XG):
                    for c in range(1, C):
                        last = nc.tensor.matmul(bank[2 + j][:, c * P:(c + 1) * P], prev[:, c - 1, j * P:(j + 1) * P],
                                                feat[:, 1, c * P:(c + 1) * P], start=True, stop=True)
                    last.then_inc(y_mm, 1)
                if not last_group:
                    group_unit(0)
                    group_unit(1)

            with turns(pe, 0, GROUPS - 1, {lo: 6, ev: 6, si: 4, bt: 1, mk: 2, xd: 3, ss: 4}):
                group(False)
            group(True)

            def out_proj():
                for j in range(2):
                    unit(bank[j][:], y_hi, y_lo, stop=False)
                    unit(bank[j][:], y_hi, y_lo, k0=KT, start=False)

            pe.wait_ge(evicted, ev.now())
            pe.wait_ge(y_lo_done, KT)
            unit(bank[0][:], y_hi, y_lo, stop=False)
            unit(bank[1][:], y_hi, y_lo, stop=False)
            norm_sum(IT)
            pe.wait_ge(y_lo_done, IT)
            unit(bank[0][:], y_hi, y_lo, k0=KT, start=False, behind={ROW_AT: norm_row})
            unit(bank[1][:], y_hi, y_lo, k0=KT, start=False)
            with turns(pe, 1, DT // 2, {lo: 4}):
                out_proj()

            def up_proj(banks, first):
                if first:
                    two_units(bank[0][:], bank[1][:])
                    unit(bank[2][:], h_hi, h_lo, halves=first, behind={SUM_AT: norm_sum_pre, ROW_AT: norm_row})
                for n in range(3 if first else 0, banks):
                    unit(bank[n][:], h_hi, h_lo)

            def down_proj(first):
                for j in range(2):
                    for n, kt in enumerate(DOWN):
                        if first and j == 0:
                            pe.wait_ge(hid_lo_done, hidden - FT + n * KT + kt)
                        unit(bank[4 + j][:], hid_hi, hid_lo, kt=kt, k0=n * KT, start=n == 0, stop=n == 2)

            hidden = 0
            for layer in range(DEPTH):
                norm_sum(DT)
                keep_warm(WARM[1])
                norm_row()
                keep_warm(WARM[2])
                if layer == 1:
                    up_proj(6, 2)
                    with turns(pe, 1, WT // 2, {lo: 6}):
                        up_proj(6, 0)
                    for n in range(4):
                        unit(bank[n][:], hid_hi, hid_lo, by_tile=None if n else (hid_lo_done, hidden))
                    with turns(pe, 1, DT // 4, {lo: 4}):
                        for n in range(4):
                            unit(bank[n][:], hid_hi, hid_lo)
                    hidden += WT
                    norm_sum(DT, 5)
                    keep_warm(WARM[1], 5)
                    norm_row()
                    keep_warm(WARM[2], 5)
                up_proj(4, 2 * layer + 1)
                with turns(pe, 1, FT // 2, {lo: 4}):
                    up_proj(4, 0)
                hidden += FT
                down_proj(True)
                with turns(pe, 1, DT // 2, {lo: 6}):
                    down_proj(False)
            norm_sum(DT)
            keep_warm(WARM[1])
            norm_row()
            keep_warm(WARM[3])
            for k in range(DT):
                pe.wait_ge(x_done, 3 * DT + k + 1)
                if k >= 4:
                    pe.wait_ge(out_ready, k - 3)
                for c in range(C):
                    last = nc.tensor.transpose(bank[k % 4][:, c * P:(c + 1) * P], xs[:, k, c * P:(c + 1) * P], ident[:])
                last.then_inc(out_turned, 1)
                if k < len(WARM_OUT):
                    keep_warm(WARM_OUT[k], 5)


_INS = ["x", "mix_pre_g", "mix_post_g", "ffn_pre_g", "ffn_post_g", "ssd_w_in", "ssd_conv_w", "ssd_conv_b", "ssd_dt_bias",
        "ssd_A_log", "ssd_D", "ssd_norm_w", "ssd_w_out", "sc_w_in", "sc_conv_w", "sc_w_out", "ffn_w_up", "ffn_conv_w",
        "ffn_conv_b", "ffn_w_down"]


def kernel(**inputs):
    import numpy as np
    import concourse.bacc as bacc
    from concourse.bass_utils import run_bass_kernel_spmd

    nc = bacc.Bacc("TRN2", target_bir_lowering=False, num_devices=1)
    arrays, args = {}, []
    for name in _INS:
        a = np.ascontiguousarray(inputs[name])
        arrays[f"in_{name}"] = a
        args.append(nc.dram_tensor(f"in_{name}", a.shape, mybir.dt.from_np(a.dtype), kind="ExternalInput").ap())
    args.append(nc.dram_tensor("out_0", inputs["x"].shape, F32, kind="ExternalOutput").ap())
    build(nc, *args)
    r = run_bass_kernel_spmd(nc, [arrays], core_ids=[0])
    return r.results[0]["out_0"]
```
